# Optimizing a Trainium2 kernel written in Bass

```python
import functools
import jax, jax.numpy as jnp
from jax import lax
import numpy as np

D_MODEL = 2048
BATCH = 1
SEQ = 256
DEPTH = 4

GRID_W = 64
CTX_LEN = 256
N_MIXERS = 3
EPS = 1e-6

F_GROUPS = 4
M_HEADS = 8
M_DQK = D_MODEL // (2 * M_HEADS)
M_DV = D_MODEL // M_HEADS
M_QK = M_HEADS * M_DQK
M_V = M_HEADS * M_DV
M_CHUNK = 64
M_IN = 2 * M_QK + 3 * M_V + 4 * M_HEADS
A_HEADS = 16
A_KV = 4
A_HD = 128
A_GROUP = A_HEADS // A_KV
A_Q = A_HEADS * A_HD
A_KVW = A_KV * A_HD
A_IN = 2 * A_Q + 2 * A_KVW
A_BLOCK = 128
A_ROT_AXIS = A_HD // 2
ROPE_THETA = 10000.0

N_FNET = (DEPTH + 2) // 3
N_MLSTM = (DEPTH + 1) // 3
N_ATTN = DEPTH // 3


def _rmsnorm(x, g):
    x32 = x.astype(jnp.float32)
    y = x32 * lax.rsqrt(jnp.mean(x32 * x32, axis=-1, keepdims=True) + EPS)
    return (y * g.astype(jnp.float32)).astype(x.dtype)

def _fourier_mix(h):
    B, T, D = h.shape
    hg = h.astype(jnp.float32).reshape(B, T, F_GROUPS, D // F_GROUPS)
    y = jnp.fft.fft2(hg, axes=(1, 3), norm='ortho').real
    return y.reshape(B, T, D).astype(h.dtype)

def _fnet_branch(h, w_gate, w_out):
    return (_fourier_mix(h) * jax.nn.silu(h @ w_gate)) @ w_out

def _mlstm_chunk(carry, xs, emit):
    C, n, m = carry
    q, k, v, ig, lf = xs
    L = lf.shape[-1]
    b = jnp.cumsum(lf, axis=-1)
    b_end = b[..., -1]
    g = b_end[..., None] - b + ig
    m_new = jnp.maximum(b_end + m, jnp.max(g, axis=-1))
    w = jnp.exp(g - m_new[..., None])
    decay = jnp.exp(b_end + m - m_new)
    C_new = decay[..., None, None] * C + jnp.einsum('bhsd,bhse->bhde', k * w[..., None], v)
    n_new = decay[..., None] * n + jnp.einsum('bhs,bhsd->bhd', w, k)
    if not emit:
        return (C_new, n_new, m_new), None
    order = jnp.tril(jnp.ones((L, L), dtype=bool))
    dmat = jnp.where(order, b[..., :, None] - b[..., None, :] + ig[..., None, :], -jnp.inf)
    inter = b + m[..., None]
    m_t = jnp.maximum(inter, jnp.max(dmat, axis=-1))
    s = jnp.einsum('bhtd,bhsd->bhts', q, k) * jnp.exp(dmat - m_t[..., None])
    a = jnp.exp(inter - m_t)
    num = a[..., None] * jnp.einsum('bhtd,bhde->bhte', q, C) + jnp.einsum('bhts,bhse->bhte', s, v)
    den = a * jnp.einsum('bhtd,bhd->bht', q, n) + jnp.sum(s, axis=-1)
    h = num / jnp.maximum(jnp.abs(den), jnp.exp(-m_t))[..., None]
    return (C_new, n_new, m_new), h

def _mlstm_scan(q, k, v, ig, lf, state, emit):
    B, NH, T, _ = q.shape
    nc = T // M_CHUNK

    def to_chunks(a):
        a = a.reshape(a.shape[:2] + (nc, M_CHUNK) + a.shape[3:])
        return jnp.moveaxis(a, 2, 0)

    xs = (to_chunks(q), to_chunks(k), to_chunks(v), to_chunks(ig), to_chunks(lf))
    state, h = lax.scan(functools.partial(_mlstm_chunk, emit=emit), state, xs)
    if emit:
        h = jnp.moveaxis(h, 0, 2).reshape(B, NH, T, M_DV)
    return state, h

def _mlstm_bidir(q, k, v, ig_f, lf_f, ig_b, lf_b, st_f, st_b, emit):
    st_f, h_f = _mlstm_scan(q, k, v, ig_f, lf_f, st_f, emit)
    flip = lambda a: jnp.flip(a, axis=2)
    st_b, h_b = _mlstm_scan(flip(q), flip(k), flip(v), flip(ig_b), flip(lf_b), st_b, emit)
    h = (h_f + flip(h_b)) if emit else None
    return st_f, st_b, h

def _mlstm_branch(h_lat, h_ctx, w_in, b_gate, hn, w_out, ctx_out):
    f32 = jnp.float32
    idx = [M_QK, 2 * M_QK, 2 * M_QK + M_V, 2 * M_QK + 2 * M_V, 2 * M_QK + 2 * M_V + 4 * M_HEADS]

    def project(h):
        B, T, _ = h.shape
        q, k, v, o, g, z = jnp.split(h @ w_in, idx, axis=-1)
        heads = lambda a, d: a.reshape(B, T, M_HEADS, d).transpose(0, 2, 1, 3).astype(f32)
        q = heads(q, M_DQK) * (M_DQK ** -0.5)
        k = heads(k, M_DQK)
        v = heads(v, M_DV)
        g = (g.astype(f32) + b_gate.astype(f32)).reshape(B, T, 4, M_HEADS).transpose(2, 0, 3, 1)
        ig_f, fg_f, ig_b, fg_b = g[0], g[1], g[2], g[3]
        scan_in = (q, k, v, ig_f, jax.nn.log_sigmoid(fg_f), ig_b, jax.nn.log_sigmoid(fg_b))
        return scan_in, o, z

    def finish(h, o, z):
        B, _, T, _ = h.shape
        h = h.transpose(0, 2, 1, 3)
        y = jax.nn.sigmoid(o.astype(f32)).reshape(B, T, M_HEADS, M_DV) * h
        y = _rmsnorm(y, hn.reshape(M_HEADS, M_DV)).reshape(B, T, M_V).astype(z.dtype)
        return (y * jax.nn.silu(z)) @ w_out

    B = h_ctx.shape[0]
    zero = (jnp.zeros((B, M_HEADS, M_DQK, M_DV), f32), jnp.zeros((B, M_HEADS, M_DQK), f32),
            jnp.zeros((B, M_HEADS), f32))
    ctx_in, o_c, z_c = project(h_ctx)
    st_f, st_b, h_c = _mlstm_bidir(*ctx_in, zero, zero, emit=ctx_out)
    lat_in, o_x, z_x = project(h_lat)
    _, _, h_x = _mlstm_bidir(*lat_in, st_f, st_b, emit=True)
    y_lat = finish(h_x, o_x, z_x)
    y_ctx = finish(h_c, o_c, z_c) if ctx_out else None
    return y_lat, y_ctx

def _rope_tables(T):
    rows = T // GRID_W
    r = jnp.repeat(jnp.arange(rows), GRID_W).astype(jnp.float32)
    col = jnp.tile(jnp.arange(GRID_W), rows).astype(jnp.float32)
    freqs = ROPE_THETA ** (-jnp.arange(0, A_ROT_AXIS, 2, dtype=jnp.float32) / A_ROT_AXIS)
    ang = jnp.concatenate([r[:, None] * freqs, col[:, None] * freqs], axis=-1)
    return jnp.cos(ang), jnp.sin(ang)

def _rope(x, cos, sin):
    x32 = x.astype(jnp.float32).reshape(x.shape[:-1] + (A_HD // 2, 2))
    x0, x1 = x32[..., 0], x32[..., 1]
    c = cos[None, :, None, :]
    s = sin[None, :, None, :]
    out = jnp.stack([x0 * c - x1 * s, x0 * s + x1 * c], axis=-1).reshape(x.shape)
    return out.astype(x.dtype)

def _attend(q, k, v):
    B, Tq = q.shape[:2]
    nb = Tq // A_BLOCK
    qb = jnp.moveaxis(q.reshape((B, nb, A_BLOCK) + q.shape[2:]), 1, 0)

    def one(qblk):
        s = jnp.einsum('bqkgd,bskd->bkgqs', qblk, k).astype(jnp.float32) * (A_HD ** -0.5)
        p = jax.nn.softmax(s, axis=-1).astype(v.dtype)
        return jnp.einsum('bkgqs,bskd->bqkgd', p, v)

    o = lax.map(one, qb)
    return jnp.moveaxis(o, 0, 1).reshape(B, Tq, A_Q)

def _attn_branch(h_lat, h_ctx, w_in, qn, kn, w_out, ctx_out):
    def project(h):
        B, T, _ = h.shape
        q, k, v, z = jnp.split(h @ w_in, [A_Q, A_Q + A_KVW, A_Q + 2 * A_KVW], axis=-1)
        q = _rmsnorm(q.reshape(B, T, A_HEADS, A_HD), qn)
        k = _rmsnorm(k.reshape(B, T, A_KV, A_HD), kn)
        v = v.reshape(B, T, A_KV, A_HD)
        return q, k, v, z

    group = lambda q: q.reshape(q.shape[:2] + (A_KV, A_GROUP, A_HD))
    qc, kc, vc, zc = project(h_ctx)
    qx, kx, vx, zx = project(h_lat)
    cos, sin = _rope_tables(h_lat.shape[1])
    qx = _rope(qx, cos, sin)
    kx = _rope(kx, cos, sin)
    k_all = jnp.concatenate([kx, kc], axis=1)
    v_all = jnp.concatenate([vx, vc], axis=1)
    y_lat = (_attend(group(qx), k_all, v_all) * jax.nn.silu(zx)) @ w_out
    y_ctx = ((_attend(group(qc), kc, vc) * jax.nn.silu(zc)) @ w_out) if ctx_out else None
    return y_lat, y_ctx

def first_inputs(seed: int = 0) -> dict:
    key = jax.random.key(seed)
    ks = jax.random.split(key, 20)
    D = D_MODEL
    nrm = lambda k, shape, s: jax.random.normal(k, shape, jnp.float32) * s
    f_bias = jnp.linspace(3.0, 6.0, M_HEADS, dtype=jnp.float32)
    base = jnp.stack([jnp.zeros_like(f_bias), f_bias, jnp.zeros_like(f_bias), f_bias])
    b_gate = (base[None] + nrm(ks[11], (N_MLSTM, 4, M_HEADS), 0.1)).reshape(N_MLSTM, 4 * M_HEADS)
    return {
        'x': nrm(ks[0], (BATCH, SEQ, D), 1.0),
        'c': nrm(ks[1], (BATCH, D), 1.0),
        'ctx': nrm(ks[2], (BATCH, CTX_LEN, D), 1.0),
        'c_ctx': nrm(ks[3], (D,), 1.0),
        'ada_w': nrm(ks[4], (DEPTH, D, 3 * D), 0.5 * D ** -0.5),
        'ada_b': nrm(ks[5], (DEPTH, 3 * D), 0.01),
        'norm_g': 1.0 + nrm(ks[6], (DEPTH, D), 0.02),
        'fnet_w_gate': nrm(ks[7], (N_FNET, D, D), D ** -0.5),
        'fnet_w_out': nrm(ks[8], (N_FNET, D, D), D ** -0.5),
        'mlstm_w_in': nrm(ks[9], (N_MLSTM, D, M_IN), D ** -0.5),
        'mlstm_b_gate': b_gate,
        'mlstm_hn': 1.0 + nrm(ks[12], (N_MLSTM, M_V), 0.02),
        'mlstm_w_out': nrm(ks[13], (N_MLSTM, M_V, D), M_V ** -0.5),
        'attn_w_in': nrm(ks[14], (N_ATTN, D, A_IN), D ** -0.5),
        'attn_qn': 1.0 + nrm(ks[15], (N_ATTN, A_HD), 0.02),
        'attn_kn': 1.0 + nrm(ks[16], (N_ATTN, A_HD), 0.02),
        'attn_w_out': nrm(ks[17], (N_ATTN, A_Q, D), A_Q ** -0.5),
        'final_g': 1.0 + nrm(ks[18], (D,), 0.02),
    }

def first_block(x, c, ctx, c_ctx, ada_w, ada_b, norm_g, fnet_w_gate, fnet_w_out, mlstm_w_in,
              mlstm_b_gate, mlstm_hn, mlstm_w_out, attn_w_in, attn_qn, attn_kn, attn_w_out, final_g):
    sc = jax.nn.silu(c)
    sc_ctx = jax.nn.silu(c_ctx)
    for i in range(DEPTH):
        kind = i % N_MIXERS
        j = i // N_MIXERS
        ctx_out = i != DEPTH - 1
        shift, scale, gate = jnp.split(sc @ ada_w[i] + ada_b[i], 3, axis=-1)
        hx = _rmsnorm(x, norm_g[i]) * (1.0 + scale[:, None]) + shift[:, None]
        hc = None
        if ctx_out or kind != 0:
            shift_c, scale_c, gate_c = jnp.split(sc_ctx @ ada_w[i] + ada_b[i], 3, axis=-1)
            hc = _rmsnorm(ctx, norm_g[i]) * (1.0 + scale_c) + shift_c
        if kind == 0:
            y_x = _fnet_branch(hx, fnet_w_gate[j], fnet_w_out[j])
            y_c = _fnet_branch(hc, fnet_w_gate[j], fnet_w_out[j]) if ctx_out else None
        elif kind == 1:
            y_x, y_c = _mlstm_branch(hx, hc, mlstm_w_in[j], mlstm_b_gate[j], mlstm_hn[j],
                                     mlstm_w_out[j], ctx_out)
        else:
            y_x, y_c = _attn_branch(hx, hc, attn_w_in[j], attn_qn[j], attn_kn[j],
                                    attn_w_out[j], ctx_out)
        x = x + gate[:, None] * y_x
        if ctx_out:
            ctx = ctx + gate_c * y_c
    return _rmsnorm(x, final_g)


DEPTH_2 = 1

N_HEADS = 16
HEAD_DIM = 64
N_KV = 4
HEADS_PER_KV = N_HEADS // N_KV
ATTN_WIDTH = N_HEADS * HEAD_DIM
KV_WIDTH = N_KV * HEAD_DIM
N_NSA_BRANCHES = 3
CMP_BLOCK = 32
CMP_STRIDE = 16
CMP_HIDDEN = 4 * HEAD_DIM
SEL_BLOCK = 64
N_SEL = 16
N_FORCED_LOCAL = 2
WINDOW = 512
Q_CHUNK = 32
FORCE_BONUS = 1e4
NEG_INF = -1e30
ROPE_THETA_2 = 500000.0
ROPE_DIM = HEAD_DIM // 4
HEAD_OUT_WIDTH = D_MODEL // N_HEADS
MAX_POS_OFFSET = 1024
POOL_WINDOWS = (2, 4, 8, 16)
POOL_GROUPS = 4
POOL_WIDTH = 1024
POOL_GROUP_WIDTH = POOL_WIDTH // POOL_GROUPS
POOL_OUT_WIDTH = D_MODEL // POOL_GROUPS
N_MERGE_BRANCHES = 2
IN_SPLITS = (ATTN_WIDTH, KV_WIDTH, KV_WIDTH, KV_WIDTH, KV_WIDTH, KV_WIDTH, KV_WIDTH,
             N_HEADS * N_NSA_BRANCHES, POOL_WIDTH, N_MERGE_BRANCHES * D_MODEL)
IN_WIDTH = ATTN_WIDTH + 6 * KV_WIDTH + N_HEADS * N_NSA_BRANCHES + POOL_WIDTH + N_MERGE_BRANCHES * D_MODEL
N_EXPERT_GROUPS = 4
EXPERTS_PER_GROUP = 4
N_EXPERTS = N_EXPERT_GROUPS * EXPERTS_PER_GROUP
TOP_K_EXPERTS = 2
D_EXPERT = 256
RMS_EPS = 1e-6


def _rms(x, g):
    xf = x.astype(jnp.float32)
    inv = lax.rsqrt(jnp.mean(xf * xf, axis=-1, keepdims=True) + RMS_EPS)
    return (xf * inv * g.astype(jnp.float32)).astype(x.dtype)

def _rope_tables_2(pos):
    inv_freq = ROPE_THETA_2 ** (-jnp.arange(0, ROPE_DIM, 2, dtype=jnp.float32) / ROPE_DIM)
    ang = pos.astype(jnp.float32)[..., None] * inv_freq
    return jnp.cos(ang)[:, :, None, :], jnp.sin(ang)[:, :, None, :]

def _partial_rope(x, cos, sin):
    half = ROPE_DIM // 2
    x1, x2, rest = x[..., :half], x[..., half:ROPE_DIM], x[..., ROPE_DIM:]
    c, s = cos.astype(x.dtype), sin.astype(x.dtype)
    return jnp.concatenate([x1 * c - x2 * s, x2 * c + x1 * s, rest], axis=-1)

def _masked_softmax(s, mask):
    s = jnp.where(mask, s.astype(jnp.float32), NEG_INF)
    return jax.nn.softmax(s, axis=-1) * mask.astype(jnp.float32)

def _compress(kv, pos_emb, w1, w2):
    B, S = kv.shape[:2]
    n_cmp = (S - CMP_BLOCK) // CMP_STRIDE + 1
    idx = np.arange(n_cmp)[:, None] * CMP_STRIDE + np.arange(CMP_BLOCK)[None, :]
    blocks = kv[:, idx] + pos_emb[None, None, :, None, :]
    flat = blocks.transpose(0, 1, 3, 2, 4).reshape(B, n_cmp, N_KV, CMP_BLOCK * HEAD_DIM)
    return jax.nn.silu(flat @ w1) @ w2

def _nsa_attention(q, kc, vc, ks, vs, kw, vw, gates):
    B, S = q.shape[:2]
    n_cmp = kc.shape[1]
    n_blk = S // SEL_BLOCK
    k_top = min(N_SEL, n_blk)
    n_chunks = S // Q_CHUNK
    scale = HEAD_DIM ** -0.5
    cmp_end = np.arange(n_cmp) * CMP_STRIDE + CMP_BLOCK - 1
    a0 = np.arange(n_cmp)[:, None] * CMP_STRIDE
    b0 = np.arange(n_blk)[None, :] * SEL_BLOCK
    ov = np.clip(np.minimum(a0 + CMP_BLOCK, b0 + SEL_BLOCK) - np.maximum(a0, b0), 0, None)
    overlap = jnp.asarray(ov / CMP_BLOCK, dtype=jnp.float32)

    kc_t, vc_t = kc.transpose(0, 2, 1, 3), vc.transpose(0, 2, 1, 3)
    ks_b = ks.reshape(B, n_blk, SEL_BLOCK, N_KV, HEAD_DIM).transpose(0, 3, 1, 2, 4)
    vs_b = vs.reshape(B, n_blk, SEL_BLOCK, N_KV, HEAD_DIM).transpose(0, 3, 1, 2, 4)
    pad = ((0, 0), (0, 0), (WINDOW, 0), (0, 0))
    kw_p = jnp.pad(kw.transpose(0, 2, 1, 3), pad)
    vw_p = jnp.pad(vw.transpose(0, 2, 1, 3), pad)
    q_ch = q.reshape(B, n_chunks, Q_CHUNK, N_KV, HEADS_PER_KV, HEAD_DIM).transpose(1, 0, 3, 4, 2, 5)
    g_ch = gates.reshape(B, n_chunks, Q_CHUNK, N_KV, HEADS_PER_KV, N_NSA_BRANCHES).transpose(1, 0, 3, 4, 2, 5)
    b_ix = jnp.arange(B)[:, None, None, None]
    g_ix = jnp.arange(N_KV)[None, :, None, None]
    blk = jnp.arange(n_blk)

    def chunk(args):
        c, qc, gc = args
        q0 = c * Q_CHUNK
        t = q0 + jnp.arange(Q_CHUNK)
        s = jnp.einsum("bgrqd,bgnd->bgrqn", qc, kc_t) * scale
        p_cmp = _masked_softmax(s, cmp_end[None, :] <= t[:, None])
        o_cmp = jnp.einsum("bgrqn,bgnd->bgrqd", p_cmp.astype(vc_t.dtype), vc_t)
        imp = jnp.einsum("bgrqn,nj->bgqj", p_cmp, overlap)
        dist = (t // SEL_BLOCK)[:, None] - blk[None, :]
        valid_blk = dist >= 0
        forced = (blk[None, :] == 0) | (valid_blk & (dist < N_FORCED_LOCAL))
        score = jnp.where(valid_blk, imp + FORCE_BONUS * forced.astype(jnp.float32), NEG_INF)
        _, sel = lax.top_k(score, k_top)
        ks_g = ks_b[b_ix, g_ix, sel].reshape(B, N_KV, Q_CHUNK, k_top * SEL_BLOCK, HEAD_DIM)
        vs_g = vs_b[b_ix, g_ix, sel].reshape(B, N_KV, Q_CHUNK, k_top * SEL_BLOCK, HEAD_DIM)
        kpos = (sel[..., None] * SEL_BLOCK + jnp.arange(SEL_BLOCK)).reshape(B, N_KV, Q_CHUNK, k_top * SEL_BLOCK)
        mask_s = (kpos <= t[:, None])[:, :, None]
        s = jnp.einsum("bgrqd,bgqkd->bgrqk", qc, ks_g) * scale
        p = _masked_softmax(s, mask_s)
        o_slc = jnp.einsum("bgrqk,bgqkd->bgrqd", p.astype(vs_g.dtype), vs_g)
        kw_c = lax.dynamic_slice_in_dim(kw_p, q0, WINDOW + Q_CHUNK, axis=2)
        vw_c = lax.dynamic_slice_in_dim(vw_p, q0, WINDOW + Q_CHUNK, axis=2)
        wpos = q0 - WINDOW + jnp.arange(WINDOW + Q_CHUNK)
        rel = t[:, None] - wpos[None, :]
        mask_w = (wpos[None, :] >= 0) & (rel >= 0) & (rel < WINDOW)
        s = jnp.einsum("bgrqd,bgkd->bgrqk", qc, kw_c) * scale
        p = _masked_softmax(s, mask_w)
        o_swa = jnp.einsum("bgrqk,bgkd->bgrqd", p.astype(vw_c.dtype), vw_c)
        return gc[..., 0:1] * o_cmp + gc[..., 1:2] * o_slc + gc[..., 2:3] * o_swa

    out = lax.map(chunk, (jnp.arange(n_chunks), q_ch, g_ch))
    return out.transpose(1, 0, 4, 2, 3, 5).reshape(B, S, N_HEADS, HEAD_DIM)

def _multiscale_pool(u):
    B, S, _ = u.shape
    ug = u.reshape(B, S, POOL_GROUPS, POOL_GROUP_WIDTH).astype(jnp.float32)
    csum = jnp.pad(jnp.cumsum(ug, axis=1), ((0, 0), (1, 0), (0, 0), (0, 0)))
    t = np.arange(S)
    outs = []
    for gi, w in enumerate(POOL_WINDOWS):
        lo = np.maximum(t + 1 - w, 0)
        cnt = jnp.asarray((t + 1 - lo).astype(np.float32))
        mean = (csum[:, t + 1, gi] - csum[:, lo, gi]) / cnt[None, :, None]
        outs.append(mean - ug[:, :, gi])
    return jnp.stack(outs, axis=2).astype(u.dtype)

def _mixer_sublayer(x, positions, attn_norm_g, w_in, q_norm_g, k_norm_cmp_g, k_norm_slc_g,
                    k_norm_swa_g, cmp_pos_emb_k, cmp_w1_k, cmp_w2_k, cmp_pos_emb_v, cmp_w1_v,
                    cmp_w2_v, w_head_out, w_pool, pool_scale, w_out):
    B, S, _ = x.shape
    h = _rms(x, attn_norm_g)
    proj = h @ w_in
    splits = np.cumsum(IN_SPLITS)[:-1].tolist()
    (q, k_cmp, v_cmp, k_slc, v_slc, k_swa, v_swa, branch_logits, pool_in,
     merge_logits) = jnp.split(proj, splits, axis=-1)
    q = q.reshape(B, S, N_HEADS, HEAD_DIM)
    kv_shape = (B, S, N_KV, HEAD_DIM)
    k_cmp, v_cmp, k_slc, v_slc, k_swa, v_swa = [a.reshape(kv_shape) for a in (k_cmp, v_cmp, k_slc, v_slc, k_swa, v_swa)]
    cos_t, sin_t = _rope_tables_2(positions)
    q = _partial_rope(_rms(q, q_norm_g), cos_t, sin_t)
    k_slc = _partial_rope(_rms(k_slc, k_norm_slc_g), cos_t, sin_t)
    k_swa = _partial_rope(_rms(k_swa, k_norm_swa_g), cos_t, sin_t)
    n_cmp = (S - CMP_BLOCK) // CMP_STRIDE + 1
    cmp_end = np.arange(n_cmp) * CMP_STRIDE + CMP_BLOCK - 1
    cos_c, sin_c = _rope_tables_2(positions[:, cmp_end])
    kc = _partial_rope(_rms(_compress(k_cmp, cmp_pos_emb_k, cmp_w1_k, cmp_w2_k), k_norm_cmp_g), cos_c, sin_c)
    vc = _compress(v_cmp, cmp_pos_emb_v, cmp_w1_v, cmp_w2_v)
    gates = jax.nn.sigmoid(branch_logits.reshape(B, S, N_HEADS, N_NSA_BRANCHES))
    o = _nsa_attention(q, kc, vc, k_slc, v_slc, k_swa, v_swa, gates)
    attn_branch = jnp.einsum("bshd,hde->bshe", o, w_head_out).reshape(B, S, D_MODEL)
    pooled = _multiscale_pool(pool_in)
    pool_branch = jnp.einsum("bsgc,gce->bsge", pooled, w_pool).reshape(B, S, D_MODEL) * pool_scale
    merge = jax.nn.sigmoid(merge_logits.reshape(B, S, N_MERGE_BRANCHES, D_MODEL))
    y = merge[:, :, 0] * attn_branch + merge[:, :, 1] * pool_branch
    return x + y @ w_out

def _moe_sublayer(x, ffn_norm_g, w_router_group, b_router_group, w_router_expert,
                  b_router_expert, w_expert_gate, w_expert_up, w_expert_down):
    B, S, D = x.shape
    ht = _rms(x, ffn_norm_g).reshape(B * S, D)
    T = ht.shape[0]
    g_prob = jax.nn.softmax((ht @ w_router_group).astype(jnp.float32) + b_router_group, axis=-1)
    p_group, g_sel = lax.top_k(g_prob, 1)
    e_logit = ((ht @ w_router_expert).astype(jnp.float32) + b_router_expert).reshape(T, N_EXPERT_GROUPS, EXPERTS_PER_GROUP)
    e_logit = e_logit[jnp.arange(T), g_sel[:, 0]]
    top_val, top_idx = lax.top_k(e_logit, TOP_K_EXPERTS)
    w_top = jax.nn.softmax(top_val, axis=-1) * p_group
    expert_id = g_sel * EXPERTS_PER_GROUP + top_idx
    combine = jnp.sum(jax.nn.one_hot(expert_id, N_EXPERTS, dtype=jnp.float32) * w_top[..., None], axis=1)
    combine = combine.astype(ht.dtype)
    y = jnp.zeros_like(ht)
    for e in range(N_EXPERTS):
        hid = jax.nn.silu(ht @ w_expert_gate[e]) * (ht @ w_expert_up[e])
        y = y + combine[:, e:e + 1] * (hid @ w_expert_down[e])
    return x + y.reshape(B, S, D)

def second_inputs(seed: int = 0) -> dict:
    key = jax.random.key(seed)
    ks = jax.random.split(key, 26)
    f32 = jnp.float32
    L = DEPTH_2

    def nrm(k, shape, fan_in):
        return jax.random.normal(k, shape, f32) * (fan_in ** -0.5)

    def gain(k, shape):
        return 1.0 + 0.05 * jax.random.normal(k, shape, f32)

    x = jax.random.normal(ks[0], (BATCH, SEQ, D_MODEL), f32)
    positions = (jax.random.randint(ks[1], (BATCH, 1), 0, MAX_POS_OFFSET, dtype=jnp.int32)
                 + jnp.arange(SEQ, dtype=jnp.int32)[None, :])
    return {
        "x": x,
        "positions": positions,
        "attn_norm_g": gain(ks[2], (L, D_MODEL)),
        "w_in": nrm(ks[3], (L, D_MODEL, IN_WIDTH), D_MODEL),
        "q_norm_g": gain(ks[4], (L, HEAD_DIM)),
        "k_norm_cmp_g": gain(ks[5], (L, HEAD_DIM)),
        "k_norm_slc_g": gain(ks[6], (L, HEAD_DIM)),
        "k_norm_swa_g": gain(ks[7], (L, HEAD_DIM)),
        "cmp_pos_emb_k": 0.02 * jax.random.normal(ks[8], (L, CMP_BLOCK, HEAD_DIM), f32),
        "cmp_w1_k": nrm(ks[9], (L, CMP_BLOCK * HEAD_DIM, CMP_HIDDEN), CMP_BLOCK * HEAD_DIM),
        "cmp_w2_k": nrm(ks[10], (L, CMP_HIDDEN, HEAD_DIM), CMP_HIDDEN),
        "cmp_pos_emb_v": 0.02 * jax.random.normal(ks[11], (L, CMP_BLOCK, HEAD_DIM), f32),
        "cmp_w1_v": nrm(ks[12], (L, CMP_BLOCK * HEAD_DIM, CMP_HIDDEN), CMP_BLOCK * HEAD_DIM),
        "cmp_w2_v": nrm(ks[13], (L, CMP_HIDDEN, HEAD_DIM), CMP_HIDDEN),
        "w_head_out": nrm(ks[14], (L, N_HEADS, HEAD_DIM, HEAD_OUT_WIDTH), HEAD_DIM),
        "w_pool": nrm(ks[15], (L, POOL_GROUPS, POOL_GROUP_WIDTH, POOL_OUT_WIDTH), POOL_GROUP_WIDTH),
        "pool_scale": gain(ks[16], (L, D_MODEL)),
        "w_out": nrm(ks[17], (L, D_MODEL, D_MODEL), D_MODEL),
        "ffn_norm_g": gain(ks[18], (L, D_MODEL)),
        "w_router_group": nrm(ks[19], (L, D_MODEL, N_EXPERT_GROUPS), D_MODEL),
        "b_router_group": 0.01 * jax.random.normal(ks[20], (L, N_EXPERT_GROUPS), f32),
        "w_router_expert": nrm(ks[21], (L, D_MODEL, N_EXPERTS), D_MODEL),
        "b_router_expert": 0.01 * jax.random.normal(ks[22], (L, N_EXPERTS), f32),
        "w_expert_gate": nrm(ks[23], (L, N_EXPERTS, D_MODEL, D_EXPERT), D_MODEL),
        "w_expert_up": nrm(ks[24], (L, N_EXPERTS, D_MODEL, D_EXPERT), D_MODEL),
        "w_expert_down": nrm(ks[25], (L, N_EXPERTS, D_EXPERT, D_MODEL), D_EXPERT),
    }

def second_block(x, positions, attn_norm_g, w_in, q_norm_g, k_norm_cmp_g, k_norm_slc_g,
              k_norm_swa_g, cmp_pos_emb_k, cmp_w1_k, cmp_w2_k, cmp_pos_emb_v, cmp_w1_v,
              cmp_w2_v, w_head_out, w_pool, pool_scale, w_out, ffn_norm_g, w_router_group,
              b_router_group, w_router_expert, b_router_expert, w_expert_gate, w_expert_up,
              w_expert_down):
    for layer in range(DEPTH_2):
        x = _mixer_sublayer(x, positions, attn_norm_g[layer], w_in[layer], q_norm_g[layer],
                            k_norm_cmp_g[layer], k_norm_slc_g[layer], k_norm_swa_g[layer],
                            cmp_pos_emb_k[layer], cmp_w1_k[layer], cmp_w2_k[layer],
                            cmp_pos_emb_v[layer], cmp_w1_v[layer], cmp_w2_v[layer],
                            w_head_out[layer], w_pool[layer], pool_scale[layer], w_out[layer])
        x = _moe_sublayer(x, ffn_norm_g[layer], w_router_group[layer], b_router_group[layer],
                          w_router_expert[layer], b_router_expert[layer], w_expert_gate[layer],
                          w_expert_up[layer], w_expert_down[layer])
    return x


def setup_inputs(seed=0):
    out = dict(first_inputs(seed))
    for name, value in second_inputs(seed + 1).items():
        if name != "x":
            out[name + "_2"] = value
    return out


def reference(
    x, c, ctx, c_ctx, ada_w, ada_b, norm_g, fnet_w_gate, fnet_w_out, mlstm_w_in, mlstm_b_gate,
    mlstm_hn, mlstm_w_out, attn_w_in, attn_qn, attn_kn, attn_w_out, final_g, positions_2,
    attn_norm_g_2, w_in_2, q_norm_g_2, k_norm_cmp_g_2, k_norm_slc_g_2, k_norm_swa_g_2,
    cmp_pos_emb_k_2, cmp_w1_k_2, cmp_w2_k_2, cmp_pos_emb_v_2, cmp_w1_v_2, cmp_w2_v_2,
    w_head_out_2, w_pool_2, pool_scale_2, w_out_2, ffn_norm_g_2, w_router_group_2,
    b_router_group_2, w_router_expert_2, b_router_expert_2, w_expert_gate_2, w_expert_up_2,
    w_expert_down_2,
):
    x = first_block(
        x, c, ctx, c_ctx, ada_w, ada_b, norm_g, fnet_w_gate, fnet_w_out, mlstm_w_in,
        mlstm_b_gate, mlstm_hn, mlstm_w_out, attn_w_in, attn_qn, attn_kn, attn_w_out, final_g,
    )
    return second_block(
        x, positions_2, attn_norm_g_2, w_in_2, q_norm_g_2, k_norm_cmp_g_2, k_norm_slc_g_2,
        k_norm_swa_g_2, cmp_pos_emb_k_2, cmp_w1_k_2, cmp_w2_k_2, cmp_pos_emb_v_2, cmp_w1_v_2,
        cmp_w2_v_2, w_head_out_2, w_pool_2, pool_scale_2, w_out_2, ffn_norm_g_2,
        w_router_group_2, b_router_group_2, w_router_expert_2, b_router_expert_2,
        w_expert_gate_2, w_expert_up_2, w_expert_down_2,
    )


_drawn_inputs = setup_inputs


def setup_inputs(seed=0):
    import zlib

    import numpy as np

    out = dict(_drawn_inputs(seed))
    spreads = {}
    factors = {'norm_g': 3.314,
     'mlstm_hn': 8.0,
     'attn_qn': 8.0,
     'attn_kn': 8.0,
     'q_norm_g_2': 8.0,
     'k_norm_cmp_g_2': 8.0,
     'k_norm_slc_g_2': 8.0,
     'k_norm_swa_g_2': 8.0,
     'cmp_pos_emb_k_2': 8.0,
     'cmp_pos_emb_v_2': 6.128,
     'b_router_group_2': 8.0,
     'b_router_expert_2': 5.835}
    for name, (base, spread) in spreads.items():
        noise = np.random.default_rng([zlib.crc32(name.encode()), seed]).standard_normal(out[name].shape)
        drawn = base * np.exp(spread * noise) if base else spread * noise
        out[name] = __import__('jax').numpy.asarray(drawn.astype(out[name].dtype))
    for name, factor in factors.items():
        out[name] = (out[name] * factor).astype(out[name].dtype)
    return out
```

```python
import numpy as np
import concourse.bass as bass
from concourse import mybir
from contextlib import ExitStack

F32 = mybir.dt.float32
I32 = mybir.dt.int32
BF16 = mybir.dt.bfloat16
ALU = mybir.AluOpType
ACT = mybir.ActivationFunctionType
AX = mybir.AxisListType.X

EPS = 1e-6
NB = 16
CTX = (0, 256)
LAT = (256, 512)
ALL = (0, 512)
TWO_PI_A = 6.28125
TWO_PI_B = 0.0019350051879882812
TWO_PI_C = float(2 * np.pi - 6.28125 - 0.0019350051879882812)
PHASES = ("ada0", "fnet0", "mlstm", "attn", "fnet3", "final", "nsa", "moe")


class Queue:

    def __init__(self, sem, serial=False):
        self.sem, self.n, self.seen, self.todo = sem, 0, {}, []
        self.serial = serial

    def wait(self, *tokens):
        for t in tokens:
            if t is not None and self.seen.get(id(t[0]), 0) < t[1]:
                self.seen[id(t[0])] = t[1]
                self.todo.append(lambda e, t=t: e.wait_ge(t[0], t[1]))

    def op(self, f, *tokens, inc=True):
        self.wait(*tokens)
        if self.serial:
            self.wait(self.last())
        if not inc:
            self.todo.append(f)
            return None
        self.n += 1
        self.todo.append(lambda e: f(e).then_inc(self.sem, 1))
        return (self.sem, self.n)

    def dma(self, out, in_, lane, *tokens):
        self.wait(*tokens)
        lane[1] += 16
        self.todo.append(lambda e: e.dma_start(out, in_).then_inc(lane[0], 16))
        return (lane[0], lane[1])

    def last(self):
        return (self.sem, self.n) if self.n else None

    def emit(self, e):
        for f in self.todo:
            f(e)


class Slot:

    def __init__(self, ap, lane=None):
        self.ap, self.lane, self.free = ap, lane, []

    def take(self):
        tokens, self.free = self.free, []
        return tokens


class Ring:
    def __init__(self, slots):
        self.slots, self.i = slots, 0

    def next(self):
        s = self.slots[self.i % len(self.slots)]
        self.i += 1
        return s


def program(nc, I, out, phases=PHASES, debug=None):
    with ExitStack() as stack:
        _program(nc, I, out, phases, debug, stack)


def _program(nc, I, out, phases, debug, stack):
    def sb(name, shape, dt=F32):
        return stack.enter_context(nc.sbuf_tensor(name, shape, dt))

    def sem(name):
        return stack.enter_context(nc.semaphore(name))

    lanes = [0]

    def lane():
        lanes[0] += 1
        return [sem(f"lane{lanes[0]}"), 0]

    XT = sb("XT", [128, NB, 512])
    HT = sb("HT", [128, NB, 512])
    YT = sb("YT", [128, NB, 512])
    R = 4
    WR = sb("WR", [128, R, 2048])
    SCB = sb("SCB", [128, 2, 2048])
    JUNK = sb("JUNK", [128, 2048], BF16)
    NAR = 13760
    AR = sb("AR", [128, NAR])
    MOD = sb("MOD", [128, 4, 48, 2])
    ADAB = sb("ADAB", [128, 4, 48])
    NG = sb("NG", [128, 4, 16])
    IDN = sb("IDN", [128, 128])
    ONE = sb("ONE", [128, 128])
    EPSC = sb("EPSC", [128, 1])
    SML = sb("SML", [128, 640])

    psum = [stack.enter_context(nc.psum_tensor(f"PS{i}", [128, 512], F32)) for i in range(8)]
    PE, SP = Queue(sem("s_pe")), Queue(sem("s_sp"))
    SA, DV, PO = (Queue(sem(n), serial=True) for n in ("s_act", "s_dve", "s_pool"))
    acc = Ring([Slot(p) for p in psum[0:4]])
    wrk = Ring([Slot(p) for p in psum[4:8]])
    wring = Ring([Slot(WR[:, i, :], lane()) for i in range(R)])

    def act(o, i, fn, *w, bias=None, scale=1.0, accum=None):
        kw = {}
        if bias is not None:
            kw["bias"] = bias
        if accum is not None:
            kw["accum_out"] = accum
        return SA.op(lambda e: e.activation(o, i, fn, scale=scale, **kw), *w)

    def tt(o, a, b, op, *w, q=None):
        return (q or DV).op(lambda e: e.tensor_tensor(o, a, b, op), *w)

    def ts(o, a, s1, s2, op0, op1, *w, q=None):
        if s2 is None:
            return (q or DV).op(lambda e: e.tensor_scalar(o, a, s1, None, op0), *w)
        return (q or DV).op(lambda e: e.tensor_scalar(o, a, s1, s2, op0, op1), *w)

    def stt(o, a, s, b, op0, op1, *w):
        return DV.op(lambda e: e.scalar_tensor_tensor(out=o, in0=a, scalar=s, in1=b, op0=op0, op1=op1), *w)

    def copy(o, a, *w, q=None):
        return (q or DV).op(lambda e: e.tensor_copy(o, a), *w)

    def recip(o, a, *w):
        return DV.op(lambda e: e.reciprocal(o, a), *w)

    def rmax(o, a, *w):
        return DV.op(lambda e: e.reduce_max(o, a, AX), *w)

    def rsum(o, a, *w):
        return DV.op(lambda e: e.reduce_sum(o, a, AX), *w)

    def mm(o, l, r, start, stop, *w, inc=False):
        return PE.op(lambda e: e.matmul(o, l, r, start=start, stop=stop), *w, inc=inc)

    def tr(o, i, *w, inc=False):
        k = i.shape[0]
        return PE.op(lambda e: e.transpose(o, i, IDN[0:k, 0:k]), *w, inc=inc)

    def load(pairs, *w):
        ln = lane()
        for o, name in pairs:
            t = PO.dma(o, I[name], ln, *w)
        return t

    mem = {"at": 0, "bar": []}

    def phase_begin():
        mem["at"] = 0
        mem["bar"] = [q.last() for q in (PE, SA, DV, PO)]

    def carve(size, shape=None, **kw):
        at = mem["at"]
        mem["at"] += size
        assert mem["at"] <= NAR, (mem["at"], NAR)
        ap = AR[:, at:at + size]
        return ap.rearrange(shape, **kw) if shape else ap

    def slot(size, shape=None, **kw):
        s = Slot(carve(size, shape, **kw))
        s.free = list(mem["bar"])
        return s

    SQR = Ring([Slot(AR[:, NAR - 512 * (i + 1):NAR - 512 * i]) for i in range(2)])
    RS = Slot(AR[:, NAR - 1536:NAR - 1024])

    tc0 = PO.op(lambda e: e.memset(ONE[:], 1.0))
    tc1 = PO.op(lambda e: e.memset(EPSC[:], EPS))
    t_c = load(((IDN[:], "ident"), (ADAB[:], "ada_b"), (NG[:], "norm_g")))
    xlane = lane()
    sclane = lane()
    t_sc = SP.dma(SCB[:], I["cc"], sclane)
    t_x = SA.dma(XT[:], I["xt"], xlane)
    for q in (PE, SA, DV):
        q.wait(tc0, tc1, t_c)

    Uf = YT[:, 0:8, :].rearrange("p a b -> p (a b)")
    Sf = SCB[:].rearrange("p a b -> p (a b)")
    t = act(Uf, Sf, ACT.Tanh, t_sc, scale=0.5)
    t = stt(Uf, Uf, 1.0, Sf, ALU.add, ALU.mult, t, t_sc)
    t_scb = ts(Sf, Uf, 0.5, None, ALU.mult, None, t)

    xtok = [t_x] * NB
    htok = [None] * NB
    ytok = [None] * NB
    hfree = []
    modtok = {}

    def ada_block(l, b):
        s = wring.next()
        tl = SP.dma(s.ap, I["ada_w"][l, b], s.lane, *s.take())
        vs = (0, 1) if l != 3 else (0,)
        for v in vs:
            o = JUNK[:] if v != vs[-1] else s.ap
            t = DV.op(lambda e, v=v, o=o: e.tensor_tensor_reduce(
                out=o, in0=s.ap, in1=SCB[:, v, :], scale=1.0, scalar=0.0, op0=ALU.mult,
                op1=ALU.add, accum_out=MOD[:, l, b, v:v + 1]), tl, t_scb)
        s.free = [t]
        return t

    def ada_finish(l, part, t):
        p = slice(16 * part, 16 * part + 16)
        for v in (0, 1) if l != 3 else (0,):
            t = tt(MOD[:, l, p, v], MOD[:, l, p, v], ADAB[:, l, p], ALU.add, t)
            if part == 1:
                t = stt(MOD[:, l, p, v], MOD[:, l, p, v], 1.0, NG[:, l, :], ALU.add, ALU.mult, t)
        modtok[l, part] = t

    def ada_thunks(l, parts=(0, 1, 2)):
        for part in parts:
            for b in range(16):
                def f(part=part, b=b):
                    t = ada_block(l, 16 * part + b)
                    if b == 15:
                        ada_finish(l, part, t)
                yield f

    background = []

    def bg(n=1):
        for _ in range(n):
            if background:
                background.pop(0)()

    def tile(src):
        s = wring.next()
        n = int(np.prod(src.shape[1:]))
        o = s.ap[:, 0:n] if n != 2048 else s.ap
        if len(src.shape) == 3:
            o = o.rearrange("p (a b) -> p a b", b=src.shape[2])
        return s, SP.dma(o, src, s.lane, *s.take())

    def proj(src, rhs, rtok, cols, M=128, K=16, ring=None):
        bank = (ring or acc).next()
        bw = bank.take()
        a, b = cols
        n = b - a
        for h in range(0, K, 16):
            s, tw = tile(src[:, h:h + 16, :] if K > 16 else src)
            w = s.ap[:, 0:16 * M].rearrange("p (k n) -> p k n", k=16)
            for k in range(16):
                t = mm(bank.ap[0:M, 0:n], w[:, k, :], rhs(h + k), h + k == 0, h + k == K - 1,
                       tw, rtok[h + k], *bw, inc=k == 15)
                bw = []
            s.free = [t]
        return bank, t

    def hproj(src, cols=ALL, M=128):
        return proj(src, lambda k: HT[:, k, cols[0]:cols[1]], htok, cols, M)

    def tproj(src, cols, N=512):
        tbs = list(range(cols[0] // 128, cols[1] // 128))
        banks = [acc.next() for _ in tbs]
        bws = [b.take() for b in banks]
        kk = 2048 // N
        for i in range(16 // kk):
            s, tw = tile(src[i])
            w = s.ap.rearrange("p (k n) -> p k n", n=N)
            for bi, tb in enumerate(tbs):
                for k in range(kk):
                    c = i * kk + k
                    t = mm(banks[bi].ap[:, 0:N], HT[:, c, 128 * tb:128 * tb + 128], w[:, k, :],
                           c == 0, c == 15, tw, htok[c], *bws[bi], inc=k == kk - 1)
                    bws[bi] = []
            s.free = [t]
        return banks, t

    stat = {}

    def square(j, cols, tok):
        a, b = cols
        s = SQR.next()
        return s, act(s.ap[:, 0:b - a], XT[:, j, a:b], ACT.Square, tok, *s.take())

    def square_sum(j, cols, s, tok):
        n = cols[1] - cols[0]
        if j == 0:
            stat["bank"] = wrk.next()
            w = stat["bank"].take()
        else:
            w = []
        t = mm(stat["bank"].ap[:, 0:n], ONE[:], s.ap[:, 0:n], j == 0, j == 15, tok, *w, inc=True)
        s.free = [t]
        stat["t"] = t

    def squares(cols):
        for j in range(NB):
            s, t = square(j, cols, xtok[j])
            square_sum(j, cols, s, t)

    def rstd(cols):
        n = cols[1] - cols[0]
        t = act(RS.ap[:, 0:n], stat["bank"].ap[:, 0:n], ACT.Sqrt, stat["t"], *RS.take(),
                bias=EPSC[:], scale=1.0 / 2048)
        stat["bank"].free = [t]
        return recip(RS.ap[:, 0:n], RS.ap[:, 0:n], t)

    def modnorm(l, cols):
        t_r = rstd(cols)
        a0 = cols[0]
        segs = [(c, v) for c, v in ((CTX, 1), (LAT, 0)) if a0 <= c[0]]
        w = list(hfree)
        for j in range(NB):
            for (a, b), v in segs:
                t = stt(HT[:, j, a:b], XT[:, j, a:b], MOD[:, l, 16 + j, v:v + 1],
                        RS.ap[:, a - a0:b - a0], ALU.mult, ALU.mult,
                        t_r, xtok[j], modtok[l, 1], *w)
                t2 = act(HT[:, j, a:b], HT[:, j, a:b], ACT.Identity, t, modtok[l, 0],
                         bias=MOD[:, l, j, v:v + 1])
            htok[j] = t2
        RS.free = [t]

    def outproj(src, l, cols, ysrc=None, K=16, half=False):
        ys = ysrc or (lambda k: YT[:, k, cols[0]:cols[1]])
        late = []
        a0 = cols[0]
        for s in SQR.slots + [RS]:
            s.free += [q.last() for q in (PE, SA, DV, PO)]
        for n in range(NB):
            bank, t = proj(src[n], ys, ytok, cols)
            for (a, b), v in ((CTX, 1), (LAT, 0)):
                if a < a0:
                    continue
                if half:
                    td = stt(XT[:, n, a:b], bank.ap[:, a - a0:b - a0], 0.5, XT[:, n, a:b],
                             ALU.mult, ALU.add, t, xtok[n])
                else:
                    td = stt(XT[:, n, a:b], bank.ap[:, a - a0:b - a0], MOD[:, l, 32 + n, v:v + 1],
                             XT[:, n, a:b], ALU.mult, ALU.add, t, modtok[l, 2], xtok[n])
            bank.free = [td]
            xtok[n] = td
            late.append((n, *square(n, cols, td)))
            if len(late) > 1:
                j, s, tq = late.pop(0)
                square_sum(j, cols, s, tq)
            bg(1)
        for j, s, tq in late:
            square_sum(j, cols, s, tq)

    def gate_silu(bank, t, dst, cols, tmp, extra=()):
        n = cols[1] - cols[0]
        ta = act(tmp.ap[:, 0:n], bank.ap[:, 0:n], ACT.Tanh, t, *tmp.take(), scale=0.5)
        td = stt(dst, tmp.ap[:, 0:n], 1.0, bank.ap[:, 0:n], ALU.add, ALU.mult, ta, *extra)
        tmp.free = [td]
        bank.free = [td]
        return td

    def fnet(l, jj, cols):
        phase_begin()
        CD = carve(2048, "p (k n) -> p k n", k=4)
        CT = carve(1536, "p (s c n) -> p s c n", s=3, c=2)
        tk = load(((CD, "dft_d"), (CT, "dft_t")), *mem["bar"])
        ab = Ring([slot(4 * 514, "p (t s n) -> p t s n", t=4, s=2) for _ in range(2)])
        tmp = Ring([slot(512) for _ in range(2)])
        a0, b0 = cols
        tbs = list(range(a0 // 128, b0 // 128))
        zt = {}
        for i, s in enumerate(ab.slots):
            z1 = DV.op(lambda e, s=s: e.memset(s.ap[:, :, 1, 0:1], 0.0), *mem["bar"])
            z2 = DV.op(lambda e, s=s: e.memset(s.ap[:, :, 1, 256:257], 0.0))
            zt[id(s)] = z2
        for g in range(4):
            A = ab.next()
            aw = A.take()
            ev = []
            for tb in tbs:
                bank = wrk.next()
                bw = bank.take()
                for k in range(4):
                    c = 4 * g + k
                    t = mm(bank.ap[:], HT[:, c, 128 * tb:128 * tb + 128], CD[:, k, :], k == 0, k == 3,
                           htok[c], tk, *bw, inc=k == 3)
                    bw = []
                t1 = act(A.ap[:, tb, 0, :], bank.ap[:, 0:257], ACT.Copy, t, *aw)
                t2 = act(A.ap[:, tb, 1, 1:256], bank.ap[:, 257:512], ACT.Copy)
                bank.free = [t2]
                ev.append(t2)
            for b in range(4):
                n = 4 * g + b
                bank, t = hproj(I["f_gate"][jj, n], cols)
                ytok[n] = gate_silu(bank, t, YT[:, n, a0:b0], cols, tmp.next(), yfree)
                bg(1)
            for b in range(4):
                n = 4 * g + b
                off = 128 * b if b < 2 else 1 + 128 * (b - 2)
                sg = 1 if b < 2 else 2
                bank = wrk.next()
                bw = bank.take()
                for si in range(len(tbs) // 2):
                    m = 0
                    for tc in range(2):
                        tb = tbs[2 * si + tc]
                        for s_, mat in ((0, 0), (1, sg)):
                            t = mm(bank.ap[:, 256 * si:256 * si + 256], A.ap[:, tb, s_, off:off + 128],
                                   CT[:, mat, tc, :], m == 0, m == 3, *ev, zt[id(A)], *bw,
                                   inc=m == 3)
                            bw = []
                            m += 1
                td = tt(YT[:, n, a0:b0], bank.ap[:, 0:b0 - a0], YT[:, n, a0:b0], ALU.mult, t, ytok[n])
                bank.free = [td]
                ytok[n] = td
            A.free = [t]
        hfree[:] = [PE.last()]
        outproj(I["f_out"][jj], l, cols)
        yfree[:] = [PE.last()]

    yfree = []

    def mlstm(l):
        phase_begin()
        bar = list(mem["bar"])
        QK = Ring([slot(1024, "p (a n) -> p a n", a=2) for _ in range(2)])
        V = Ring([slot(4 * 257, "p (t n) -> p t n", t=4) for _ in range(2)])
        O = Ring([slot(1024, "p (t n) -> p t n", t=4) for _ in range(2)])
        C = carve(512)
        CB = slot(1024, "p (d n) -> p d n", d=2)
        HH = slot(1024, "p (t n) -> p t n", t=4)
        pat = mem["at"]
        P = Ring([Slot(carve(1536)), Slot(carve(1536))])
        IG, LF, CU, MX = (AR[:, pat + 512 * i:pat + 512 * i + 512] for i in range(4))
        E1 = AR[:, pat + 2048:pat + 2560]
        ACOL = SML[:, 0:160].rearrange("p (t r) -> p t r", t=4)
        ECOL = SML[:, 160:320].rearrange("p (t r) -> p t r", t=4)
        GB = SML[:, 320:321]
        HN = SML[:, 321:337]
        ST = Ring([Slot(SML[:, 340 + 16 * i:356 + 16 * i]) for i in range(4)])
        t_g = load(((GB, "m_bg"), (HN, "m_hn")), *bar)
        t_hn = ts(HN, HN, 0.5, None, ALU.mult, None, t_g)
        for s in V.slots:
            t_one = DV.op(lambda e, s=s: e.memset(s.ap[:, :, 256:257], 1.0), *bar)
        bank, t = hproj(I["m_g"])
        r = slice(0, 40)
        a = act(IG[r], bank.ap[0:40, :], ACT.Identity, t, t_g, *bar, bias=GB[0:40])
        f = act(LF[r], bank.ap[64:104, :], ACT.Identity, bias=GB[64:104])
        bank.free = [f]
        e = act(E1[r], LF[r], ACT.Abs, f)
        e = act(E1[r], E1[r], ACT.Exp, e, scale=-1.0)
        e = act(E1[r], E1[r], ACT.Ln, e, bias=ONE[r, 0:1])
        t = ts(LF[r], LF[r], 0.0, None, ALU.min, None, e)
        t = tt(LF[r], LF[r], E1[r], ALU.subtract, t, e)
        z = DV.op(lambda e_: e_.memset(E1[r], 0.0), t)

        def scan(o, d1, op1, *w):
            t1 = DV.op(lambda e_: e_.tensor_tensor_scan(o[0:8], LF[0:8], d1[0:8], 0.0, ALU.add, op1), *w)
            t2 = DV.op(lambda e_: e_.tensor_tensor_scan(
                o[32:40, 0:256][:, ::-1], LF[32:40, 0:256][:, ::-1], d1[32:40, 0:256][:, ::-1],
                0.0, ALU.add, op1), *w)
            return DV.op(lambda e_: e_.tensor_tensor_scan(
                o[32:40, 256:512][:, ::-1], LF[32:40, 256:512][:, ::-1], d1[32:40, 256:512][:, ::-1],
                o[32:40, 0:1], ALU.add, op1), t2, t1)

        zc = DV.op(lambda e_: e_.memset(CU[r], 0.0), *bar)
        zm = DV.op(lambda e_: e_.memset(MX[r], 0.0), *bar)
        t_cu = scan(CU, E1, ALU.add, z, t, zc)
        t_mx = scan(MX, IG, ALU.max, t, a, zm)
        t_c = tt(C[r], CU[r], MX[r], ALU.subtract, t_cu, t_mx)
        t_a = tt(IG[r], IG[r], CU[r], ALU.subtract, t_cu, t_mx)
        t_e = act(MX[r], MX[r], ACT.Exp, t_c, scale=-1.0)
        bank = wrk.next()
        bw = bank.take()
        for tb in range(4):
            t = tr(bank.ap[:, 40 * tb:40 * tb + 40], IG[r, 128 * tb:128 * tb + 128], t_a, *bw)
            bw = []
        for tb in range(4):
            t = tr(bank.ap[:, 160 + 40 * tb:200 + 40 * tb], MX[r, 128 * tb:128 * tb + 128], t_e,
                   inc=tb == 3)
        t1 = copy(SML[:, 0:320], bank.ap[:, 0:320], t)
        bank.free = [t1]
        t_col = t1
        for s in P.slots:
            s.free = [t_a, t_e, t, t_c]

        heads = {}

        def project(h):
            qk, v, o = QK.next(), V.next(), O.next()
            qw, vw, ow = qk.take(), v.take(), o.take()
            st = heads[h] = dict(qk=qk, v=v, o=o)

            def q_():
                bank, t = hproj(I["m_q"][h])
                st["tq"] = act(qk.ap[:, 0, :], bank.ap[:], ACT.Copy, t, *qw, scale=float(128 ** -0.5))
                bank.free = [st["tq"]]

            def k_():
                bank, t = hproj(I["m_k"][h])
                st["tk"] = act(qk.ap[:, 1, :], bank.ap[:], ACT.Copy, t, *qw)
                bank.free = [st["tk"]]

            def vo():
                banks, t = tproj(I["m_vo"][h], ALL)
                for tb, b in enumerate(banks):
                    t1 = act(o.ap[:, tb, :], b.ap[:, 256:512], ACT.Tanh, t, *ow, scale=0.5)
                    t2 = copy(v.ap[:, tb, 0:256], b.ap[:, 0:256], t, t1, t_one, *vw)
                    b.free = [t1, t2]
                st["tv"] = t2
                st["to"] = ts(o.ap[:], o.ap[:], 0.5, 0.5, ALU.mult, ALU.add, t1, q=PO)

            def z_(b):
                n = 2 * h + b
                bank, t = hproj(I["m_z"][n])
                ytok[n] = gate_silu(bank, t, YT[:, n, :], ALL, E2.next(), yfree)
            return [q_, k_, vo, lambda: z_(0), lambda: z_(1)]

        E2 = Ring([slot(512)])
        fill = []

        def go(n=1):
            for _ in range(n):
                if fill:
                    fill.pop(0)()
                    bg(1)

        span = {(0, 0): (0, 512), (1, 0): (128, 512), (2, 0): (256, 512), (3, 0): (384, 512),
                (0, 1): None, (1, 1): (0, 512), (2, 1): (256, 384), (3, 1): (256, 512)}

        def attend(h):
            st = heads[h]
            qk, v, o = st["qk"], st["v"], st["o"]
            cw = CB.take()
            tcb = []
            for d in range(2):
                bank = wrk.next()
                row = 32 * d + h
                t = mm(bank.ap[:], IDN[0:40, row:row + 1].to_broadcast([40, 128]), C[0:40, :],
                       True, True, t_c, *bank.take(), inc=True)
                ta = act(CB.ap[:, d, :], bank.ap[:], ACT.Copy, t, *cw)
                bank.free = [ta]
                tcb.append(ta)
            pcol = [0, 512, 1024, 1280]
            ptok = {}
            Ps = [P.next(), P.next()]
            Pw = [p.take() for p in Ps]
            for sbk in range(4):
                c0, c1 = (0, 512) if sbk < 2 else (256, 512)
                bank = wrk.next()
                t = mm(bank.ap[:, 0:c1 - c0], qk.ap[:, 1, 128 * sbk:128 * sbk + 128],
                       qk.ap[:, 0, c0:c1], True, True, st["tq"], st["tk"], *bank.take(), inc=True)
                go(1) if sbk in (0, 2) else None
                fr = []
                for d in range(2):
                    p = Ps[d].ap[:, pcol[sbk]:pcol[sbk] + c1 - c0]
                    ta = ts(p, CB.ap[:, d, c0:c1], ACOL[:, sbk, 32 * d + h:32 * d + h + 1], 0.0,
                            ALU.add, ALU.min, tcb[d], t_col, *Pw[d])
                    ta = act(p, p, ACT.Exp, ta)
                    g0 = 128 * sbk - c0
                    pd = p[:, g0:g0 + 128]
                    tm = PO.op(lambda e, pd=pd, sg=1 if d == 0 else -1: e.affine_select(
                        out=pd, in_=pd, compare_op=ALU.is_ge, fill=0.0, base=0,
                        pattern=[[sg, 128]], channel_multiplier=-sg), ta)
                    tm = tt(p, p, bank.ap[:, 0:c1 - c0], ALU.mult, tm, t)
                    ptok[sbk, d] = tm
                    fr.append(tm)
                bank.free = fr
            hw = HH.take()
            use = {0: ([0], [0, 1]), 1: ([0, 1], [1]), 2: ([0, 1, 2], [0, 1, 2, 3]),
                   3: ([0, 1, 2, 3], [0, 1, 3])}
            for tb in range(4):
                for d in range(2):
                    bank = wrk.next()
                    bw = bank.take()
                    ks = use[tb][d]
                    for i, s_ in enumerate(ks):
                        c = pcol[s_] + 128 * tb - (0 if s_ < 2 else 256)
                        t = mm(bank.ap[:, 0:257], Ps[d].ap[:, c:c + 128], v.ap[:, s_, :], i == 0,
                               i == len(ks) - 1, ptok[s_, d], st["tv"], *bw, inc=i == len(ks) - 1)
                        bw = []
                    Ps[d].free.append(t)
                    s = ST.next()
                    den = bank.ap[:, 256:257]
                    t1 = stt(s.ap[:, 0:1], den, -1.0, ECOL[:, tb, 32 * d + h:32 * d + h + 1],
                             ALU.mult, ALU.max, t, t_col, *s.take())
                    t1 = tt(s.ap[:, 0:1], den, s.ap[:, 0:1], ALU.max, t1)
                    t1 = recip(s.ap[:, 0:1], s.ap[:, 0:1], t1)
                    if d == 0:
                        t1 = ts(HH.ap[:, tb, :], bank.ap[:, 0:256], s.ap[:, 0:1], None, ALU.mult,
                                None, t1, *hw)
                    else:
                        t1 = stt(HH.ap[:, tb, :], bank.ap[:, 0:256], s.ap[:, 0:1], HH.ap[:, tb, :],
                                 ALU.mult, ALU.add, t1, th)
                    th = t1
                    s.free = [t1]
                    bank.free = [t1]
            CB.free = [DV.last()]
            v.free = [PE.last()]
            qk.free = [PE.last()]
            s = ST.next()
            ty = tt(HH.ap[:], HH.ap[:], o.ap[:], ALU.mult, th, st["to"])
            sq = E2.next()
            w = sq.take()
            for tb in range(4):
                t1 = act(sq.ap[:, 0:256], HH.ap[:, tb, :], ACT.Square, ty, *s.free, *w,
                         accum=s.ap[:, tb:tb + 1])
            sq.free = [t1]
            t1 = act(s.ap[:, 4:8], s.ap[:, 0:4], ACT.Sqrt, t1, bias=EPSC[:], scale=1.0 / 256)
            t1 = recip(s.ap[:, 4:8], s.ap[:, 4:8], t1)
            o.free = [ty]
            yn = []
            for tb in range(4):
                yn.append(ts(HH.ap[:, tb, :], HH.ap[:, tb, :], s.ap[:, 4 + tb:5 + tb], None,
                             ALU.mult, None, t1, sq.free[0]))
            s.free = [yn[-1]]
            go(1)
            for b in range(2):
                bank = wrk.next()
                bw = bank.take()
                for tb in range(4):
                    t = tr(bank.ap[:, 128 * tb:128 * tb + 128], HH.ap[:, tb, 128 * b:128 * b + 128],
                           yn[tb], *bw, inc=tb == 3)
                    bw = []
                n = 2 * h + b
                td = stt(YT[:, n, :], bank.ap[:], HN[:, n:n + 1], YT[:, n, :], ALU.mult, ALU.mult,
                         t, ytok[n], t_hn)
                bank.free = [td]
                ytok[n] = td
            HH.free = [t]

        fill += project(0)
        go(9)
        for h in range(8):
            if h < 7:
                fill += project(h + 1)
            attend(h)
            go(9)
        hfree[:] = [PE.last()]
        outproj(I["m_out"], l, ALL)
        yfree[:] = [PE.last()]

    def attn(l):
        phase_begin()
        bar = list(mem["bar"])
        VT = carve(2048, "p (t n) -> p t n", t=4)
        KT = carve(2048, "p (g n) -> p g n", g=4)
        QT = Ring([slot(512), slot(512)])
        SQ, QG, RQ, T1 = slot(512), slot(512), slot(512), slot(512)
        PM = slot(1536)
        PT = slot(1536)
        TZ = slot(512)
        ROT = SML[:, 0:128]
        COS = carve(256)
        SIN = carve(256)
        QN = SML[:, 128:130]
        ST = Ring([Slot(SML[:, 140 + 16 * i:156 + 16 * i]) for i in range(4)])
        tk = load(((ROT, "rot1"), (COS, "cos1"), (SIN, "sin1"), (QN, "qkn")), *bar)

        def rope_norm(bank, t, dst, gain, extra):
            t1 = act(SQ.ap, bank.ap[:], ACT.Square, t, *SQ.take())
            t2 = act(QG.ap, bank.ap[:], ACT.Copy, t, tk, *QG.take(), scale=gain)
            bank.free = [t2]
            b1, b2 = wrk.next(), wrk.next()
            t1 = mm(b1.ap[:], ONE[:], SQ.ap, True, True, t1, *b1.take(), inc=True)
            SQ.free = [t1]
            t3 = mm(b2.ap[:, 0:256], ROT, QG.ap[:, 256:512], True, True, t2, tk, *b2.take(), inc=True)
            t1 = act(RQ.ap, b1.ap[:], ACT.Sqrt, t1, *RQ.take(), bias=EPSC[:], scale=1.0 / 128)
            b1.free = [t1]
            t1 = recip(RQ.ap, RQ.ap, t1)
            t4 = tt(T1.ap[:, 0:256], b2.ap[:, 0:256], SIN, ALU.mult, t3, tk, *T1.take())
            b2.free = [t4]
            t5 = tt(QG.ap[:, 256:512], QG.ap[:, 256:512], COS, ALU.mult, t3)
            t5 = tt(QG.ap[:, 256:512], QG.ap[:, 256:512], T1.ap[:, 0:256], ALU.add, t4, t5)
            T1.free = [t5]
            t5 = tt(dst, QG.ap, RQ.ap, ALU.mult, t5, t1, *extra)
            QG.free = [t5]
            RQ.free = [t5]
            return t5

        banks, t = tproj(I["a_v"], ALL)
        for tb, b in enumerate(banks):
            tv = copy(VT[:, tb, :], b.ap[:], t, *bar)
            b.free = [tv]
        ktok = []
        for g in range(4):
            bank, t = hproj(I["a_k"][g])
            ktok.append(rope_norm(bank, t, KT[:, g, :], QN[:, 1:2], bar))
            bg(1)
        qs = {}
        fill = []

        def go(n=1):
            for _ in range(n):
                if fill:
                    fill.pop(0)()
                    bg(1)

        def project(h):
            def q_():
                bank, t = hproj(I["a_q"][h])
                q = QT.next()
                qs[h] = (q, rope_norm(bank, t, q.ap, QN[:, 0:1], q.take()))

            def z_():
                bank, t = hproj(I["a_z"][h])
                ytok[h] = gate_silu(bank, t, YT[:, h, :], ALL, TZ, yfree)
            return [q_, z_]

        sc = float(128 ** -0.5)
        where = {0: (0, 256), 1: (256, 256), 2: (512, 512), 3: (1024, 512)}

        def attend(h):
            g = h // 4
            q, tq = qs[h]
            pw = PM.take()
            b0 = wrk.next()
            bw = b0.take()
            for tb in range(2):
                t = mm(b0.ap[:, 256 * tb:256 * tb + 256], q.ap[:, 128 * tb:128 * tb + 128],
                       KT[:, g, 0:256], True, True, tq, ktok[g], *bw, inc=True)
                bw = []
            bs = [(b0, 0, t), (b0, 256, t)]
            for tb in (2, 3):
                b = wrk.next()
                t = mm(b.ap[:], q.ap[:, 128 * tb:128 * tb + 128], KT[:, g, :], True, True, *b.take(),
                       inc=True)
                bs.append((b, 0, t))
            q.free = [t]
            pt = []
            for tb in range(4):
                b, c0, t = bs[tb]
                at, n = where[tb]
                s = ST.next()
                sa = s.ap
                t1 = rmax(sa[:, 0:1], b.ap[:, c0:c0 + n], t, *s.take())
                t1 = ts(sa[:, 1:2], sa[:, 0:1], -sc, None, ALU.mult, None, t1)
                t1 = act(PM.ap[:, at:at + n], b.ap[:, c0:c0 + n], ACT.Exp, t1, *pw, bias=sa[:, 1:2],
                         scale=sc, accum=sa[:, 2:3])
                b.free = [t1]
                t2 = recip(sa[:, 3:4], sa[:, 2:3], t1)
                t2 = ts(PM.ap[:, at:at + n], PM.ap[:, at:at + n], sa[:, 3:4], None, ALU.mult, None, t2)
                s.free = [t2]
                pt.append(t2)
            go(1)
            pw = PT.take()
            te = []
            for i in range(3):
                b = wrk.next()
                bw = b.take()
                if i < 2:
                    jobs = [(tb, i) for tb in range(4)]
                else:
                    jobs = [(2, 2), (3, 2), (2, 3), (3, 3)]
                for m, (tb, s_) in enumerate(jobs):
                    at = where[tb][0] + 128 * s_
                    t = tr(b.ap[:, 128 * m:128 * m + 128], PM.ap[:, at:at + 128], pt[tb], *bw,
                           inc=m == 3)
                    bw = []
                if i % 2:
                    te.append(act(PT.ap[:, 512 * i:512 * i + 512], b.ap[:], ACT.Copy, t, *pw))
                else:
                    te.append(copy(PT.ap[:, 512 * i:512 * i + 512], b.ap[:], t, *pw))
                b.free = [te[-1]]
            PM.free = [t]
            go(1)
            b = wrk.next()
            bw = b.take()
            for s_ in range(4):
                vv = VT[:, s_, 128 * g:128 * g + 128]
                if s_ < 2:
                    o_, r_ = b.ap[:], PT.ap[:, 512 * s_:512 * s_ + 512]
                else:
                    o_, r_ = b.ap[:, 256:512], PT.ap[:, 512 + 256 * s_:768 + 256 * s_]
                t = mm(o_, vv, r_, s_ == 0, s_ == 3, *te, tv, *bw, inc=s_ == 3)
                bw = []
            PT.free = [t]
            td = stt(YT[:, h, :], b.ap[:], 0.5, YT[:, h, :], ALU.mult, ALU.mult, t, ytok[h])
            b.free = [td]
            ytok[h] = td

        fill += project(0)
        go(9)
        for h in range(16):
            if h < 15:
                fill += project(h + 1)
            attend(h)
            go(9)
        hfree[:] = [PE.last()]
        outproj(I["a_out"], l, ALL)
        yfree[:] = [PE.last()]

    def gainnorm(cols, gain, tg, dst, wfree=()):
        t_r = rstd(cols)
        a, b = cols
        toks = []
        for j in range(NB):
            toks.append(stt(dst[:, j, a:b], XT[:, j, a:b], gain[:, j:j + 1], RS.ap[:, 0:b - a],
                            ALU.mult, ALU.mult, t_r, tg, xtok[j], *wfree))
        RS.free = [toks[-1]]
        return toks

    GN = SML[:, 592:640]

    def nsa():
        phase_begin()
        bar = list(mem["bar"])
        a0, b0 = LAT
        c = LAT
        QB = carve(2048, "p (n t) -> p n t", n=8)
        KD = [carve(1024, "p (g t) -> p g t", g=4) for _ in range(2)]
        T2K, T2V = KD
        VV = carve(1024, "p (t n) -> p t n", t=2)
        KR = Ring([Slot(XT[:, 12 + 2 * i:14 + 2 * i, 0:256]) for i in range(2)])
        for s in KR.slots:
            s.free = list(bar)
        COS, SIN = carve(256), carve(256)
        SQ, QG, RQ, T1 = slot(256), slot(256), slot(256), slot(256)
        PM = slot(1024)
        CMP = carve(480, "p (t n) -> p t n", t=2)
        POOLW = Ring([slot(272) for _ in range(3)])
        OT = slot(256)
        WHO = carve(1024, "p (n e) -> p n e", n=8)
        PL = XT[:, 0:8, 0:256]
        PT = Slot(XT[:, 8:12, 0:256])
        PT.free = list(bar)
        KC = SML[:, 0:60]
        VC = SML[:, 60:316].rearrange("p (g d) -> p g d", g=4)
        CST = carve(272)
        KN = SML[:, 316:320]
        PSC = SML[:, 320:336]
        GT = SML[:, 336:432].rearrange("p (t n) -> p t n", t=2)
        W2 = carve(2 * 128 + 2 * 64)
        POS = carve(32, "p (a j) -> p a j", a=2)
        ST = Ring([Slot(SML[:, 432 + 16 * i:448 + 16 * i]) for i in range(8)])
        HID = [carve(120, "p (b n) -> p b n", b=2) for _ in range(2)]
        B64, ROT = CST[:, 0:128], CST[:, 128:256]
        INV = CST[:, 256:257]
        tk = load(((CST[:, 0:257], "nsa_c"), (KN, "nsa_kn"), (PSC, "pool_s"), (WHO, "w_ho"),
                   (W2, "w2"), (POS, "pos")), *bar)
        PI_ = PM.ap[:, 0:256].bitcast(I32)
        PF, KF, RR = PM.ap[:, 256:512], PM.ap[:, 512:768], PM.ap[:, 768:1024]
        t = load(((PI_, "positions"),), *bar)
        t = copy(PF, PI_, t)
        t = ts(PF, PF, INV, None, ALU.mult, None, t)
        t = ts(PI_, PF, float(1 / (2 * np.pi)), None, ALU.mult, None, t)
        t = copy(KF, PI_, t)
        t = stt(RR, KF, -TWO_PI_A, PF, ALU.mult, ALU.add, t)
        t = stt(RR, KF, -TWO_PI_B, RR, ALU.mult, ALU.add, t)
        t = stt(RR, KF, -TWO_PI_C, RR, ALU.mult, ALU.add, t)
        PIF = 3.1415925
        t = ts(RR, RR, PIF, -PIF, ALU.min, ALU.max, t)
        t_s = act(SIN, RR, ACT.Sin, t)
        t = act(KF, RR, ACT.Abs, t)
        t = ts(KF, KF, -1.0, float(np.pi / 2), ALU.mult, ALU.add, t)
        t_cs = act(COS, KF, ACT.Sin, t)
        PM.free = [t_cs]
        CC = [carve(60, "p (g n) -> p g n", g=4) for _ in range(2)]
        for g in range(4):
            tcc = copy(CC[0][:, g, :], COS[:, 31::16], t_cs, t_s, *bar)
            tcc = copy(CC[1][:, g, :], SIN[:, 31::16])

        def rope_norm(src, sfree, t, dst, gain, extra, n=256, cs=None):
            co, si = cs or (COS, SIN)
            t1 = act(SQ.ap[:, 0:n], src, ACT.Square, t, *SQ.take())
            t2 = act(QG.ap[:, 0:n], src, ACT.Copy, t, tk, *QG.take(), scale=gain)
            if sfree is not None:
                sfree.free = [t2]
            b1, b2 = wrk.next(), wrk.next()
            t1 = mm(b1.ap[:, 0:n], B64, SQ.ap[:, 0:n], True, True, t1, tk, *b1.take(), inc=True)
            SQ.free = [t1]
            t3 = mm(b2.ap[:, 0:n], ROT, QG.ap[:, 0:n], True, True, t2, tk, *b2.take(), inc=True)
            t1 = act(RQ.ap[:, 0:n], b1.ap[:, 0:n], ACT.Sqrt, t1, *RQ.take(), bias=EPSC[:],
                     scale=1.0 / 64)
            b1.free = [t1]
            t1 = recip(RQ.ap[:, 0:n], RQ.ap[:, 0:n], t1)
            t4 = tt(T1.ap[:, 0:n], b2.ap[:, 0:n], si, ALU.mult, t3, t_cs, t_s, tcc, *T1.take())
            b2.free = [t4]
            t5 = tt(QG.ap[:, 0:n], QG.ap[:, 0:n], co, ALU.mult, t3)
            t5 = tt(QG.ap[:, 0:n], QG.ap[:, 0:n], T1.ap[:, 0:n], ALU.add, t4, t5)
            T1.free = [t5]
            t5 = tt(dst, QG.ap[:, 0:n], RQ.ap[:, 0:n], ALU.mult, t5, t1, *extra)
            QG.free = [t5]
            RQ.free = [t5]
            return t5

        t2tok = []
        for i, (name, T2) in enumerate((("n_kc", T2K), ("n_vc", T2V))):
            dlane = lane()
            kr = KR.next()
            kw = kr.take()
            for b in range(2):
                bank, t = hproj(I[name][b], c)
                t1 = copy(kr.ap[:, b, :], bank.ap[:, 0:256], t, *kw)
                bank.free = [t1]
            for par in range(2):
                td = PO.dma(T2[0:64, par::2, :], kr.ap[64 * par:64 * par + 64, :, :], dlane, t1, *bar)
                td = PO.dma(T2[64:128, par::2, 0:255], kr.ap[64 * par:64 * par + 64, :, 1:256], dlane)
            kr.free = [td]
            t2tok.append(td)
        for n in range(4):
            bank, t = hproj(I["n_q"][n], c)
            tq = rope_norm(bank.ap[:, 0:256], bank, t, QB[:, n, :], KN[:, 0:1], bar)
        vcw = []
        for i, T2 in enumerate((T2K, T2V)):
            w1s = []
            for hb in range(2):
                w1s.append(tile(I["n_w1"][i, hb]))
            MV = YT[:, 8:10, :].rearrange("p a b -> p (a b)")[:, 0:976].rearrange("p (j n) -> p j n", j=16) if i == 0 else \
                YT[:, 10:12, :].rearrange("p a b -> p (a b)")[:, 0:976].rearrange("p (j n) -> p j n", j=16)
            for u in range(2):
                for g in range(4):
                    src = T2[:, g, :].rearrange("p (m r) -> p m r", r=16)[:, u:u + 15, 0:16:2]
                    dst = MV[:, 8 * u:8 * u + 8, 15 * g:15 * g + 15].rearrange("p r n -> p n r")
                    t = copy(dst, src, t2tok[i], *yfree)
            t = copy(MV[:, :, 60:61], POS[:, i, :].rearrange("p (j a) -> p j a", a=1), tk)
            for hb in range(2):
                s, tw = w1s[hb]
                w = s.ap.rearrange("p (k n) -> p k n", k=16)
                bank = acc.next()
                bw = bank.take()
                for j in range(16):
                    tm_ = mm(bank.ap[:, 0:61], w[:, j, :], MV[:, j, :], j == 0, j == 15, t, tw, *bw,
                             inc=j == 15)
                    bw = []
                s.free = [tm_]
                st = ST.next()
                ta = act(st.ap[:, 0:1], bank.ap[:, 60:61], ACT.Copy, tm_, *st.take())
                hd = HID[i][:, hb, :]
                x1 = T1.ap[:, 0:60]
                tb_ = ts(x1, bank.ap[:, 0:60], st.ap[:, 0:1], None, ALU.add, None, ta, *T1.take())
                bank.free = [tb_]
                st.free = [tb_]
                ta = act(hd, x1, ACT.Tanh, tb_, *bar, scale=0.5)
                ta = stt(hd, hd, 1.0, x1, ALU.add, ALU.mult, ta)
                T1.free = [ta]
            if i == 0:
                bank = acc.next()
                bw = bank.take()
                for hb in range(2):
                    t = mm(bank.ap[:, 0:60], W2[:, 128 * hb:128 * hb + 128], HID[0][:, hb, :], hb == 0,
                           hb == 1, ta, tk, *bw, inc=hb == 1)
                    bw = []
                x1 = POOLW.slots[0]
                t = act(x1.ap[:, 0:60], bank.ap[:, 0:60], ACT.Copy, t, *x1.take(), scale=0.5)
                bank.free = [t]
                fl = lambda z: z.rearrange("p g n -> p (g n)")
                t_kc = rope_norm(x1.ap[:, 0:60], x1, t, KC, KN[:, 1:2], bar, n=60,
                                 cs=(fl(CC[0]), fl(CC[1])))
            else:
                bank = acc.next()
                bw = bank.take()
                for g in range(4):
                    for hb in range(2):
                        t = mm(bank.ap[0:15, 64 * g:64 * g + 64], HID[1][:, hb, 15 * g:15 * g + 15],
                               W2[:, 256 + 64 * hb:320 + 64 * hb], hb == 0, hb == 1, ta, tk, *bw,
                               inc=hb == 1)
                        bw = []
                t_vc = act(SML[0:15, 60:316], bank.ap[0:15, 0:256], ACT.Copy, t, *bar, scale=0.5)
                bank.free = [t_vc]
        mvread = PE.last()
        ktok = []
        for i, name in enumerate(("n_ks", "n_kw")):
            dlane = lane()
            kr = KR.next()
            kw = kr.take()
            for b in range(2):
                bank, t = hproj(I[name][b], c)
                t1 = rope_norm(bank.ap[:, 0:256], bank, t, kr.ap[:, b, :], KN[:, 2 + i:3 + i], kw)
            for par in range(2):
                for half in range(2):
                    td = PO.dma(KD[i][64 * half:64 * half + 64, par::2, :],
                                kr.ap[64 * par:64 * par + 64, :, :], dlane, t1, DV.last())
            kr.free = [td]
            ktok.append(td)
        banks, t = tproj(I["n_v"], c)
        for tb, b in enumerate(banks):
            tv = copy(VV[:, tb, :], b.ap[:], t, *bar)
            b.free = [tv]
        bank, t = hproj(I["n_g"], c, M=48)
        gtmp = POOLW.slots[1]
        t = act(gtmp.ap[0:48, 0:256], bank.ap[0:48, 0:256], ACT.Tanh, t, *gtmp.take(), scale=0.5)
        bank.free = [t]
        t = ts(gtmp.ap[0:48, 0:256], gtmp.ap[0:48, 0:256], 0.5, 0.5, ALU.mult, ALU.add, t)
        bank = wrk.next()
        bw = bank.take()
        for tb in range(2):
            t2 = tr(bank.ap[:, 48 * tb:48 * tb + 48], gtmp.ap[0:48, 128 * tb:128 * tb + 128], t, *bw,
                    inc=tb == 1)
            bw = []
        t_gt = copy(SML[:, 336:432], bank.ap[:, 0:96], t2, *bar)
        bank.free = [t_gt]
        gtmp.free = [t2]
        for n in range(4, 8):
            bank, t = hproj(I["n_q"][n], c)
            tq = rope_norm(bank.ap[:, 0:256], bank, t, QB[:, n, :], KN[:, 0:1], bar)
        t_q = tq

        isc = 0.125
        M3 = lambda ap: ap.rearrange("p (h n) -> p h n", h=16)
        for tb in range(2):
            banks = [wrk.next(), wrk.next()]
            pc = CMP[:, tb, :]
            for par in range(2):
                bw = banks[par].take()
                b = 64 * par
                for i in range(8):
                    g = i // 2
                    t = mm(banks[par].ap[:, 15 * i:15 * i + 15],
                           QB[b:b + 64, i, 128 * tb:128 * tb + 128],
                           KC[b:b + 64, 15 * g:15 * g + 15], True, True, t_q, t_kc, *bw, inc=i == 7)
                    bw = []
                t = tt(CMP[:, tb, 120 * par:120 * par + 120], banks[par].ap[:, 0:120],
                       CMADD(tb)[:, 0:120], ALU.add, t, t_cm[0])
                banks[par].free = [t]
            s = T1.ap[:, 0:16]
            t = rmax(s, M3(pc), t, *T1.take())
            t = tt(M3(pc), M3(pc), s.rearrange("p (h a) -> p h a", a=1).to_broadcast([128, 16, 15]),
                   ALU.subtract, t)
            t = act(pc, pc, ACT.Exp, t, scale=isc)
            t = rsum(s, M3(pc), t)
            t = recip(s, s, t)
            for par in range(2):
                t = tt(s[:, 8 * par:8 * par + 8], s[:, 8 * par:8 * par + 8], GT[:, tb, 3 * par:48:6],
                       ALU.mult, t, t_gt)
            t = tt(M3(pc), M3(pc), s.rearrange("p (h a) -> p h a", a=1).to_broadcast([128, 16, 15]),
                   ALU.mult, t)
            t = tt(pc, pc, CMMUL(tb), ALU.mult, t)
            T1.free = [t]
            t_cmp = t

        fill = []

        def go(n=1):
            for _ in range(n):
                if fill:
                    fill.pop(0)()

        mtok = [[None] * NB, [None] * NB]
        pltok = [None] * 8

        def merge(n, w):
            def f():
                bank, t = hproj(I["n_m"][16 * w + n], c)
                o = YT[:, n, 256:512] if w == 0 else YT[:, n, 0:256]
                mtok[w][n] = act(o, bank.ap[:, 0:256], ACT.Tanh, t, mvread, *yfree, scale=0.5)
                bank.free = [mtok[w][n]]
            return f

        def pool(n):
            def f():
                bank, t = hproj(I["n_p"][n], c)
                steps = n // 2 + 1
                u, a, b = POOLW.slots
                w = u.take() + a.take() + b.take()
                t1 = PO.op(lambda e: e.memset(u.ap[:, 0:16], 0.0), *w)
                t2 = PO.op(lambda e: e.memset(a.ap[:, 0:16], 0.0))
                t3 = PO.op(lambda e: e.memset(b.ap[:, 0:16], 0.0))
                t = copy(u.ap[:, 16:272], bank.ap[:, 0:256], t, *w)
                bank.free = [t]
                cur, k = u, 1
                for i in range(steps):
                    nxt = a if i % 2 == 0 else b
                    t = tt(nxt.ap[:, 16:272], cur.ap[:, 16:272], cur.ap[:, 16 - k:272 - k], ALU.add,
                           t, t1, t2, t3, q=PO)
                    cur, k = nxt, 2 * k
                t = tt(cur.ap[:, 16:272], cur.ap[:, 16:272], CNT(n // 2), ALU.mult, t, t_cm[0], q=PO)
                t = tt(PL[:, n, :], cur.ap[:, 16:272], u.ap[:, 16:272], ALU.subtract, t, *bar, q=PO)
                for s in POOLW.slots:
                    s.free = [t]
                pltok[n] = t
            return f

        def poolout(n):
            def f():
                g = n // 4
                s, tw = None, None
                if n % 8 == 0:
                    pw["s"], pw["t"] = tile(I["w_pool"][n // 8])
                s, tw = pw["s"], pw["t"]
                w = s.ap.rearrange("p (n k e) -> p n k e", n=8, k=2)
                bank = acc.next()
                bw = bank.take()
                for k in range(2):
                    t = mm(bank.ap[:, 0:256], w[:, n % 8, k, :], PL[:, 2 * g + k, :], k == 0, k == 1,
                           pltok[2 * g + k], tw, *bw, inc=k == 1)
                    bw = []
                if n % 8 == 7:
                    s.free = [t]
                x = QG
                t = act(x.ap, bank.ap[:, 0:256], ACT.Copy, t, tk, *x.take(), scale=PSC[:, n:n + 1])
                bank.free = [t]
                t = stt(YT[:, n, 0:256], YT[:, n, 0:256], 1.0, x.ap, ALU.add, ALU.mult, t, mtok[1][n])
                x.free = [t]
                mtok[1][n] = t
            return f

        pw = {}
        for n in range(8):
            fill.append(merge(2 * n, 0))
            fill.append(merge(2 * n + 1, 0))
            fill.append(pool(n))
        fill += [merge(n, 1) for n in range(16)]
        late = [poolout(n) for n in range(16)]
        ow = {}

        def attend(h):
            g, b, blk = h // 4, 64 * (h % 2), h // 2
            ch = 8 * (h % 2) + h // 2
            P = PM.ap.rearrange("p (t x) -> p t x", t=2)
            pw_ = PM.take()
            toks = []
            sbank = []
            for tb in range(2):
                n = 128 * (tb + 1)
                bank = wrk.next()
                bw = bank.take()
                for br in range(2):
                    t = mm(bank.ap[:, n * br:n * br + n], QB[b:b + 64, blk, 128 * tb:128 * tb + 128],
                           KD[br][b:b + 64, g, 0:n], True, True, t_q, ktok[br], *bw, inc=br == 1)
                    bw = []
                sbank.append((bank, t))
            for tb in range(2):
                n = 128 * (tb + 1)
                bank, t = sbank[tb]
                pp = P[:, tb, 0:2 * n]
                t = tt(pp, bank.ap[:, 0:2 * n], MASK(tb), ALU.add, t, t_cm[0], *pw_)
                bank.free = [t]
                s = ST.next()
                sa = s.ap
                t = rmax(sa[:, 0:2], pp.rearrange("p (r n) -> p r n", r=2), t, *s.take())
                t = ts(sa[:, 2:4], sa[:, 0:2], -isc, None, ALU.mult, None, t)
                for br in range(2):
                    t1 = act(P[:, tb, n * br:n * br + n], P[:, tb, n * br:n * br + n], ACT.Exp, t,
                             bias=sa[:, 2 + br:3 + br], scale=isc, accum=sa[:, 4 + br:5 + br])
                t = recip(sa[:, 6:8], sa[:, 4:6], t1)
                t = tt(sa[:, 6:8], sa[:, 6:8], GT[:, tb, 3 * h + 1:3 * h + 3], ALU.mult, t, t_gt)
                for br in range(2):
                    t1 = ts(P[:, tb, n * br:n * br + n], P[:, tb, n * br:n * br + n],
                            sa[:, 6 + br:7 + br], None, ALU.mult, None, t)
                s.free = [t1]
                toks.append(t1)
            go(1)
            A, B = wrk.next(), wrk.next()
            aw, bw = A.take(), B.take()
            for br in range(2):
                tr(A.ap[:, 256 * br:256 * br + 128], P[:, 0, 128 * br:128 * br + 128], toks[0], *aw)
                aw = []
                t = tr(A.ap[:, 256 * br + 128:256 * br + 256], P[:, 1, 256 * br:256 * br + 128],
                       toks[1], inc=br == 1)
            ta_ = t
            for br in range(2):
                t = tr(B.ap[:, 128 * br:128 * br + 128], P[:, 1, 256 * br + 128:256 * br + 256], *bw)
                bw = []
            for tb in range(2):
                t = tr(B.ap[0:15, 256 + 128 * tb:384 + 128 * tb], CMP[:, tb, 15 * ch:15 * ch + 15],
                       t_cmp, inc=tb == 1)
            PM.free = [t]
            X = PT.ap
            xw = PT.take()
            t1 = act(X[:, 0:2, :], A.ap.rearrange("p (a b) -> p a b", a=2), ACT.Copy, ta_, *xw)
            t2 = copy(X[:, 2, :], B.ap[:, 0:256], t, *xw)
            t3 = copy(X[0:15, 3, :], B.ap[0:15, 256:512])
            A.free, B.free = [t1], [t3]
            go(1)
            if h % 2 == 0:
                ow["bank"] = acc.next()
                bw = ow["bank"].take()
            else:
                bw = []
            ob = ow["bank"].ap
            for br in range(2):
                mm(ob[b:b + 64, 0:256], VV[:, 0, 256 * br + 64 * g:256 * br + 64 * g + 64],
                   X[:, br, :], br == 0, False, t1, t3, tv, *bw)
                bw = []
                mm(ob[b:b + 64, 128:256], VV[:, 1, 256 * br + 64 * g:256 * br + 64 * g + 64],
                   X[:, 2, 128 * br:128 * br + 128], False, False)
            t = mm(ob[b:b + 64, 0:256], VC[0:15, g, :], X[0:15, 3, :], False, True, t_vc, inc=True)
            PT.free = [t]
            if h % 2:
                t = copy(OT.ap, ob[:, 0:256], t, *OT.take())
                ow["bank"].free = [t]
                for i in range(2):
                    hh = h - 1 + i
                    bank = wrk.next()
                    tm_ = mm(bank.ap[:, 0:256], WHO[64 * i:64 * i + 64, blk, :],
                             OT.ap[64 * i:64 * i + 64, :], True, True, t, tk, *bank.take(), inc=True)
                    OT.free = [tm_]
                    td = stt(YT[:, hh, 256:512], YT[:, hh, 256:512], 1.0, bank.ap[:, 0:256],
                             ALU.add, ALU.mult, tm_, mtok[0][hh])
                    bank.free = [td]
                    mtok[0][hh] = td
            go(1)

        for h in range(16):
            attend(h)
        go(99)
        hfree[:] = [PE.last()]
        for n in range(16):
            late[n]()
            ytok[n] = tt(YT[:, n, 256:512], YT[:, n, 256:512], YT[:, n, 0:256], ALU.add, mtok[0][n],
                         mtok[1][n])
        outproj(I["n_out"], None, LAT, half=True)
        yfree[:] = [PE.last()]

    HL = HT[:, :, 0:256]
    t_cm = [None]

    def CMADD(tb):
        return HT[:, 4 + tb, 0:240]

    def CMMUL(tb):
        return HT[:, 6 + tb, 0:240]

    def CNT(i):
        return HT[:, 8 + i, 0:256]

    def MASK(tb):
        if tb:
            return MK[:, 0:512]
        return MK[:, 512:768]

    MK = SCB[:].rearrange("p a b -> p (a b)")

    def load_masks():
        w = [q.last() for q in (PE, SA, DV, PO)]
        t_cm[0] = load(((HT[:, 4:6, 0:240], "cm_add"), (HT[:, 6:8, 0:240], "cm_mul"),
                        (HT[:, 8:12, 0:256], "cnt"), (MK[:, 0:768], "masks")), *w)

    def moe():
        phase_begin()
        bar = list(mem["bar"])
        c = LAT
        YF = YT[:].rearrange("p a (b n) -> p (a b) n", n=256)
        LG = carve(256)
        RB = SML[:, 0:1]
        CMB = carve(32, "p (t e) -> p t e", t=2)
        CR = carve(256)
        CBC = Ring([slot(256), slot(256)])
        TG = Ring([slot(256), slot(256)])
        UU = Ring([slot(256), slot(256)])
        IDX = SML[:, 4:8]
        S = SML[:, 16:80]
        t_b = load(((RB, "r_b"), (IDX, "idx4")), *bar)
        bank, t = hproj(I["r_w"], c, M=20)
        t = act(LG[0:20], bank.ap[0:20, 0:256], ACT.Identity, t, t_b, *bar, bias=RB[0:20])
        bank.free = [t]
        bank = wrk.next()
        bw = bank.take()
        for tb in range(2):
            t2 = tr(bank.ap[:, 20 * tb:20 * tb + 20], LG[0:20, 128 * tb:128 * tb + 128], t, *bw,
                    inc=tb == 1)
            bw = []
        LT = carve(40, "p (t n) -> p t n", t=2)
        t = copy(AR[:, mem["at"] - 40:mem["at"]], bank.ap[:, 0:40], t2)
        bank.free = [t]
        lt = t

        def first_max(oh, x, m, tmp, mt, *w):
            t = ts(oh, x, m, None, ALU.is_equal, None, *w)
            t = tt(tmp, oh, IDX, ALU.mult, t)
            t = rmax(mt, tmp, t)
            return ts(oh, tmp, mt, None, ALU.is_equal, None, t)

        for tb in range(2):
            G = LT[:, tb, 0:4]
            v = lambda a, n: S[:, a:a + n]
            t = rmax(v(0, 1), G, t)
            t = ts(v(1, 1), v(0, 1), -1.0, None, ALU.mult, None, t)
            t = act(v(4, 4), G, ACT.Exp, t, bias=v(1, 1), accum=v(2, 1))
            t = recip(v(3, 1), v(2, 1), t)
            t = rmax(v(0, 1), v(4, 4), t)
            t = first_max(v(8, 4), v(4, 4), v(0, 1), v(12, 4), v(1, 1), t)
            t = ts(v(16, 4), LT[:, tb, 4:8], v(8, 1), None, ALU.mult, None, t)
            for g in range(1, 4):
                t = stt(v(16, 4), LT[:, tb, 4 + 4 * g:8 + 4 * g], v(8 + g, 1), v(16, 4), ALU.mult,
                        ALU.add, t)
            t = rmax(v(0, 1), v(16, 4), t)
            t = first_max(v(20, 4), v(16, 4), v(0, 1), v(12, 4), v(1, 1), t)
            t = stt(v(24, 4), v(20, 4), -1e30, v(16, 4), ALU.mult, ALU.add, t)
            t = rmax(v(28, 1), v(24, 4), t)
            t = first_max(v(32, 4), v(24, 4), v(28, 1), v(12, 4), v(1, 1), t)
            t = tt(v(29, 1), v(28, 1), v(0, 1), ALU.subtract, t)
            t = act(v(29, 1), v(29, 1), ACT.Exp, t)
            t = ts(v(30, 1), v(29, 1), 1.0, None, ALU.add, None, t)
            t = recip(v(30, 1), v(30, 1), t)
            t = tt(v(30, 1), v(30, 1), v(3, 1), ALU.mult, t)
            t = tt(v(31, 1), v(30, 1), v(29, 1), ALU.mult, t)
            t = ts(v(36, 4), v(20, 4), v(30, 1), None, ALU.mult, None, t)
            t = stt(v(36, 4), v(32, 4), v(31, 1), v(36, 4), ALU.mult, ALU.add, t)
            for g in range(4):
                t = ts(CMB[:, tb, 4 * g:4 * g + 4], v(36, 4), v(8 + g, 1), None, ALU.mult, None, t)
        bank = wrk.next()
        bw = bank.take()
        for tb in range(2):
            t2 = tr(bank.ap[0:16, 128 * tb:128 * tb + 128], CMB[:, tb, :], t, *bw, inc=tb == 1)
            bw = []
        t_cr = copy(CR[0:16], bank.ap[0:16, 0:256], t2)
        bank.free = [t_cr]
        order = {"e": {}}

        def spread(e):
            b = wrk.next()
            t = mm(b.ap[:, 0:256], IDN[0:16, e:e + 1].to_broadcast([16, 128]), CR[0:16, :], True,
                   True, t_cr, *b.take(), inc=True)
            s = CBC.next()
            t = act(s.ap, b.ap[:, 0:256], ACT.Copy, t, *s.take())
            b.free = [t]
            order["e"][e] = (s, t)

        for n in range(32):
            e, f = n // 2, n % 2
            gb, tg = hproj(I["e_g"][e, f], c)
            ub, tu = hproj(I["e_u"][e, f], c)
            if f == 0:
                spread(e)
            s, tc = order["e"][e]
            g, u = TG.next(), UU.next()
            ta = act(g.ap, gb.ap[:, 0:256], ACT.Tanh, tg, *g.take(), scale=0.5)
            t1 = stt(g.ap, g.ap, 1.0, gb.ap[:, 0:256], ALU.add, ALU.mult, ta)
            gb.free = [t1]
            t2 = tt(u.ap, ub.ap[:, 0:256], s.ap, ALU.mult, tu, tc, *u.take())
            ub.free = [t2]
            t3 = tt(YF[:, n, :], g.ap, u.ap, ALU.mult, t1, t2, *yfree)
            g.free, u.free = [t3], [t3]
            ytok2[n] = t3
            if f == 1:
                s.free = [t2]
        for n in range(NB):
            bank, t = proj(I["e_d"][n], lambda k: YF[:, k, :], ytok2, c, K=32)
            td = stt(XT[:, n, 256:512], bank.ap[:, 0:256], 0.5, XT[:, n, 256:512], ALU.mult, ALU.add,
                     t, xtok[n])
            bank.free = [td]
            xtok[n] = td
            outs.append(SA.dma(out[n], XT[:, n, 256:512], olane, td))

    ytok2 = [None] * 32
    olane = lane()
    outs = []

    if "ada0" in phases:
        for f in ada_thunks(0, (1, 0)):
            f()
        background.extend(ada_thunks(0, (2,)))
    elif debug:
        need = [l for l, p in enumerate(("fnet0", "mlstm", "attn", "fnet3")) if p in phases]
        for l in need:
            for f in ada_thunks(l):
                f()
    if "ada0" in phases:
        for l in (1, 2, 3):
            background.extend(ada_thunks(l))
    if "fnet0" in phases:
        squares(ALL)
        modnorm(0, ALL)
        while background and (0, 2) not in modtok:
            bg(1)
        fnet(0, 0, ALL)
    elif "mlstm" in phases or "attn" in phases:
        squares(ALL)

    def settle(l):
        while background and (l, 2) not in modtok:
            bg(1)

    if "mlstm" in phases:
        settle(1)
        modnorm(1, ALL)
        mlstm(1)
    if "attn" in phases:
        settle(2)
        modnorm(2, ALL)
        attn(2)
    if "fnet3" in phases:
        settle(3)
        squares(LAT)
        modnorm(3, LAT)
        fnet(3, 1, LAT)
    if "nsa" in phases:
        load_masks()
        tg = load(((GN, "gains"),), *[q.last() for q in (PE, SA, DV, PO)])
        if "final" in phases:
            if "fnet3" not in phases:
                squares(LAT)
            xtok[:] = gainnorm(LAT, GN[:, 0:16], tg, XT)
        squares(LAT)
        htok[:] = gainnorm(LAT, GN[:, 16:32], tg, HT, hfree)
        nsa()
    if "moe" in phases:
        tg = load(((GN, "gains"),), *[q.last() for q in (PE, SA, DV, PO)])
        if "nsa" not in phases:
            squares(LAT)
        htok[:] = gainnorm(LAT, GN[:, 32:48], tg, HT, hfree)
        moe()
    elif debug:
        for n in range(NB):
            outs.append(SA.dma(out[n], XT[:, n, 256:512], olane, xtok[n]))
    if debug == "ctx":
        for n in range(NB):
            outs.append(SA.dma(I["dbg"][n], XT[:, n, 0:256], olane, xtok[n]))
    SA.wait(outs[-1])

    block = stack.enter_context(nc.Block())
    block.tensor(lambda e: PE.emit(e))
    block.scalar(lambda e: SA.emit(e))
    block.vector(lambda e: DV.emit(e))
    block.gpsimd(lambda e: PO.emit(e))
    block.sync(lambda e: SP.emit(e))


def _blocks(w, n=128):
    k, m = w.shape
    return np.ascontiguousarray(w.reshape(k // 128, 128, m // n, n).transpose(2, 1, 0, 3))


def _rows(w, kk=4):
    k, m = w.shape
    return np.ascontiguousarray(w.reshape(k // 128 // kk, kk, 128, m).transpose(0, 2, 1, 3))


def _col(v):
    v = v.reshape(v.shape[:-1] + (v.shape[-1] // 128, 128))
    return np.ascontiguousarray(np.moveaxis(v, -1, 0))


def _fourier_order():
    one = np.concatenate([np.arange(256), 511 - np.arange(256)])
    return np.concatenate([512 * g + one for g in range(4)])


def _constants():
    C = {}
    f = np.float32
    C["ident"] = np.eye(128, dtype=f)
    d = np.arange(512)[:, None]
    cosd = np.cos(2 * np.pi * ((d * np.arange(257)) % 512) / 512) / np.sqrt(512)
    sind = np.sin(2 * np.pi * ((d * np.arange(1, 256)) % 512) / 512) / np.sqrt(512)
    cd = np.concatenate([cosd, sind], 1).reshape(4, 128, 512).transpose(1, 0, 2)
    C["dft_d"] = np.ascontiguousarray(cd).astype(f)
    t = np.arange(256)
    ph = 2 * np.pi * (np.outer(t, t) % 256) / 256
    ct, st = np.cos(ph) / 32, np.sin(ph) / 32
    m = np.stack([ct, -st, st]).reshape(3, 2, 128, 256).transpose(2, 0, 1, 3)
    C["dft_t"] = np.ascontiguousarray(m).astype(f)
    r = np.zeros((128, 128), f)
    for i in range(64):
        r[2 * i + 1, 2 * i] = -1
        r[2 * i, 2 * i + 1] = 1
    C["rot1"] = r
    freqs = f(10000.0) ** (-np.arange(0, 64, 2, dtype=f) / f(64))
    rr = np.repeat(np.arange(4), 64).astype(f)
    cc = np.tile(np.arange(64), 4).astype(f)
    ang = np.concatenate([rr[:, None] * freqs, cc[:, None] * freqs], -1)
    C["cos1"] = np.ascontiguousarray(np.repeat(np.cos(ang), 2, axis=1).T).astype(f)
    C["sin1"] = np.ascontiguousarray(np.repeat(np.sin(ang), 2, axis=1).T).astype(f)
    nc_ = np.zeros((128, 257), f)
    nc_[0:64, 0:64] = 1
    nc_[64:128, 64:128] = 1
    for b in (0, 64):
        for i in range(8):
            nc_[b + 8 + i, 128 + b + i] = -1
            nc_[b + i, 128 + b + 8 + i] = 1
    inv = f(500000.0) ** (-np.arange(0, 16, 2, dtype=f) / f(16))
    for b in (0, 64):
        nc_[b:b + 8, 256] = inv
        nc_[b + 8:b + 16, 256] = inv
    C["nsa_c"] = nc_
    tt_ = np.arange(256).reshape(2, 128).T
    ok = (np.arange(15) * 16 + 31)[None, None, :] <= tt_[:, :, None]
    C["cm_add"] = np.tile(np.where(ok, 0.0, -1e30), (1, 1, 16)).astype(f)
    C["cm_mul"] = np.tile(ok, (1, 1, 16)).astype(f)
    C["cnt"] = np.broadcast_to(np.stack([1.0 / np.minimum(t + 1, w) for w in (2, 4, 8, 16)]),
                               (128, 4, 256)).astype(f)
    p = np.arange(128)[:, None]
    low = np.where(np.arange(128)[None] <= p, 0.0, -1e30)
    full = np.zeros((128, 128))
    C["masks"] = np.concatenate([full, low, full, low, low, low], 1).astype(f)
    C["idx4"] = np.broadcast_to(np.array([4.0, 3.0, 2.0, 1.0], f), (128, 4)).copy()
    return {k: np.ascontiguousarray(v) for k, v in C.items()}


def layout(x, c, ctx, c_ctx, ada_w, ada_b, norm_g, fnet_w_gate, fnet_w_out, mlstm_w_in,
           mlstm_b_gate, mlstm_hn, mlstm_w_out, attn_w_in, attn_qn, attn_kn, attn_w_out, final_g,
           positions_2, attn_norm_g_2, w_in_2, q_norm_g_2, k_norm_cmp_g_2, k_norm_slc_g_2,
           k_norm_swa_g_2, cmp_pos_emb_k_2, cmp_w1_k_2, cmp_w2_k_2, cmp_pos_emb_v_2, cmp_w1_v_2,
           cmp_w2_v_2, w_head_out_2, w_pool_2, pool_scale_2, w_out_2, ffn_norm_g_2,
           w_router_group_2, b_router_group_2, w_router_expert_2, b_router_expert_2,
           w_expert_gate_2, w_expert_up_2, w_expert_down_2):
    A = _constants()
    con = np.ascontiguousarray
    xt = np.concatenate([ctx[0], x[0]], 0)
    A["xt"] = con(xt.T.reshape(16, 128, 512).transpose(1, 0, 2))
    A["cc"] = con(np.broadcast_to(np.stack([c[0], c_ctx]), (128, 2, 2048)))
    A["ada_w"] = con(ada_w.transpose(0, 2, 1).reshape(4, 48, 128, 2048))
    A["ada_b"] = _col(ada_b)
    A["norm_g"] = _col(norm_g)
    o = _fourier_order()
    A["f_gate"] = np.stack([_blocks(w[:, o]) for w in fnet_w_gate])
    A["f_out"] = np.stack([_blocks(w[o]) for w in fnet_w_out])
    w = mlstm_w_in[0]
    A["m_q"] = _blocks(w[:, 0:1024])
    A["m_k"] = _blocks(w[:, 1024:2048])
    v, og = w[:, 2048:4096], w[:, 4096:6144]
    A["m_vo"] = np.stack([_rows(np.concatenate([v[:, 256 * h:256 * h + 256],
                                                og[:, 256 * h:256 * h + 256]], 1)) for h in range(8)])
    g = w[:, 6144:6176]
    gp = np.zeros((2048, 128), w.dtype)
    bp = np.zeros((128, 1), mlstm_b_gate.dtype)
    for at, src in ((0, 0), (64, 8), (32, 16), (96, 24)):
        gp[:, at:at + 8] = g[:, src:src + 8]
        bp[at:at + 8, 0] = mlstm_b_gate[0, src:src + 8]
    A["m_g"] = _blocks(gp)[0]
    A["m_bg"] = bp
    A["m_z"] = _blocks(w[:, 6176:])
    A["m_hn"] = _col(mlstm_hn[0])
    A["m_out"] = _blocks(mlstm_w_out[0])
    w = attn_w_in[0]
    A["a_q"] = _blocks(w[:, 0:2048])
    A["a_k"] = _blocks(w[:, 2048:2560])
    A["a_v"] = _rows(w[:, 2560:3072])
    A["a_z"] = _blocks(w[:, 3072:])
    A["qkn"] = con(np.stack([attn_qn[0], attn_kn[0]], 1))
    A["a_out"] = _blocks(attn_w_out[0])
    A["gains"] = con(np.concatenate([_col(final_g), _col(attn_norm_g_2[0]), _col(ffn_norm_g_2[0])], 1))
    w = w_in_2[0]
    at = [0]

    def cut(n):
        at[0] += n
        return w[:, at[0] - n:at[0]]

    A["n_q"] = _blocks(cut(1024))
    A["n_kc"], A["n_vc"] = _blocks(cut(256)), _blocks(cut(256))
    ks, vs, kw, vw = cut(256), cut(256), cut(256), cut(256)
    A["n_ks"], A["n_kw"] = _blocks(ks), _blocks(kw)
    A["n_v"] = _rows(np.concatenate([vs, vw], 1))
    A["n_g"] = _blocks(cut(48), 48)[0]
    A["n_p"] = _blocks(cut(1024))
    A["n_m"] = _blocks(cut(4096))
    two = lambda v_: np.concatenate([v_, v_])
    A["nsa_kn"] = con(np.stack([two(q_norm_g_2[0]), two(k_norm_cmp_g_2[0]), two(k_norm_slc_g_2[0]),
                                two(k_norm_swa_g_2[0])], 1))
    A["positions"] = con(np.broadcast_to(positions_2, (128, 256)))
    A["pos"] = con(np.stack([p_[0].reshape(16, 128).T for p_ in (cmp_pos_emb_k_2, cmp_pos_emb_v_2)], 1))
    A["n_w1"] = np.stack([_blocks(w_[0]) for w_ in (cmp_w1_k_2, cmp_w1_v_2)])
    k2 = cmp_w2_k_2[0].reshape(2, 128, 64)
    v2 = cmp_w2_v_2[0].reshape(2, 128, 64)
    A["w2"] = con(np.concatenate([k2[0], k2[0], k2[1], k2[1], v2[0], v2[1]], 1))
    A["w_ho"] = con(w_head_out_2[0].reshape(8, 128, 128).transpose(1, 0, 2))
    wp = w_pool_2[0].reshape(4, 2, 128, 4, 128)
    A["w_pool"] = con(wp.transpose(0, 3, 2, 1, 4).reshape(2, 8, 128, 2, 128).transpose(0, 2, 1, 3, 4)
                      .reshape(2, 128, 2048))
    A["pool_s"] = _col(pool_scale_2[0])
    A["n_out"] = _blocks(w_out_2[0])
    A["r_w"] = _blocks(np.concatenate([w_router_group_2[0], w_router_expert_2[0]], 1), 20)[0]
    rb = np.zeros((128, 1), b_router_group_2.dtype)
    rb[0:4, 0] = b_router_group_2[0]
    rb[4:20, 0] = b_router_expert_2[0]
    A["r_b"] = rb
    A["e_g"] = np.stack([_blocks(w_) for w_ in w_expert_gate_2[0]])
    A["e_u"] = np.stack([_blocks(w_) for w_ in w_expert_up_2[0]])
    A["e_d"] = _blocks(w_expert_down_2[0].reshape(4096, 2048))
    return A


def kernel(**inputs):
    import concourse.bacc as _bacc
    from concourse.bass_utils import run_bass_kernel_spmd as _run

    arrays = layout(**{k: np.asarray(v) for k, v in inputs.items()})
    nc = _bacc.Bacc("TRN2", target_bir_lowering=False, num_devices=1)
    aps = {k: nc.dram_tensor(k, a.shape, mybir.dt.from_np(a.dtype), kind="ExternalInput").ap()
           for k, a in arrays.items()}
    out = nc.dram_tensor("out", (16, 128, 256), F32, kind="ExternalOutput").ap()
    program(nc, aps, out)
    r = _run(nc, [arrays], core_ids=[0])
    y = r.results[0]["out"]
    return np.ascontiguousarray(y.reshape(2048, 256).T)[None]
```

```python
import numpy as np
import concourse.bass as bass
from concourse import mybir
from contextlib import ExitStack

F32 = mybir.dt.float32
I32 = mybir.dt.int32
F32R = mybir.dt.float32r
BF16 = mybir.dt.bfloat16
ALU = mybir.AluOpType
ACT = mybir.ActivationFunctionType
AX = mybir.AxisListType.X

EPS = 1e-6
NB = 16
CTX = (0, 256)
LAT = (256, 512)
ALL = (0, 512)
TWO_PI_A = 6.28125
TWO_PI_B = 0.0019350051879882812
TWO_PI_C = float(2 * np.pi - 6.28125 - 0.0019350051879882812)
NPE = 13
PHASES = ("ada0", "fnet0", "mlstm", "attn", "fnet3", "final", "nsa", "moe")


class Queue:

    def __init__(self, sem, serial=False):
        self.sem, self.n, self.seen, self.todo = sem, 0, {}, []
        self.serial = serial

    def wait(self, *tokens):
        for t in tokens:
            if t is not None and self.seen.get(id(t[0]), 0) < t[1]:
                self.seen[id(t[0])] = t[1]
                self.todo.append(lambda e, t=t: e.wait_ge(t[0], t[1]))

    def op(self, f, *tokens, inc=True, chain=True):
        self.wait(*tokens)
        if self.serial and chain:
            self.wait(self.last())
        if not inc:
            self.todo.append(f)
            return None
        self.n += 1
        self.todo.append(lambda e: f(e).then_inc(self.sem, 1))
        return (self.sem, self.n)

    def dma(self, out, in_, lane, *tokens):
        self.wait(*tokens)
        lane[1] += 16
        self.todo.append(lambda e: e.dma_start(out, in_).then_inc(lane[0], 16))
        return (lane[0], lane[1])

    def last(self):
        return (self.sem, self.n) if self.n else None

    def emit(self, e):
        for f in self.todo:
            f(e)


class Slot:

    def __init__(self, ap, lane=None):
        self.ap, self.lane, self.free, self.turn, self.held = ap, lane, [], 0, False

    def take(self):
        tokens, self.free = self.free, []
        return tokens


class Ring:
    def __init__(self, slots):
        self.slots, self.i = slots, 0

    def next(self):
        while self.slots[self.i % len(self.slots)].held:
            self.i += 1
        s = self.slots[self.i % len(self.slots)]
        self.i += 1
        return s


def program(nc, I, out, phases=PHASES, debug=None):
    with ExitStack() as stack:
        _program(nc, I, out, phases, debug, stack)


def _program(nc, I, out, phases, debug, stack):
    def sb(name, shape, dt=F32):
        return stack.enter_context(nc.sbuf_tensor(name, shape, dt))

    def sem(name):
        return stack.enter_context(nc.semaphore(name))

    sems = []
    XD = nc.dram_tensor("xd", (NB, 128, 512), F32, kind="Internal").ap()
    HH_ = sb("HTH", [128, NB, 512], F32R)
    HL_ = sb("HTL", [128, NB, 512], F32R)
    YT = sb("YT", [128, NB, 512])
    R, NP = 4, 3
    WR = sb("WR", [128, R, 1024])
    WH = sb("WH", [128, NP, 1024], F32R)
    WL = sb("WL", [128, NP, 1024], F32R)
    SCB = sb("SCB", [128, 2, 2048])
    JUNK = sb("JUNK", [128, 768])
    NAR = 11792
    AR = sb("AR", [128, NAR])
    MOD = sb("MOD", [128, 4, 48, 2])
    ADAB = sb("ADAB", [128, 4, 48])
    NG = sb("NG", [128, 4, 16])
    IDN = sb("IDN", [128, 128])
    ONE = sb("ONE", [128, 128])
    EPSC = sb("EPSC", [128, 1])
    SML = sb("SML", [128, 640])

    psum = [stack.enter_context(nc.psum_tensor(f"PS{i}", [128, 512], F32)) for i in range(8)]
    esem = [sem(n) for n in ("s_pe", "s_sp", "s_act", "s_dve", "s_pool")]
    T = dict(YT=YT, HH_=HH_, HL_=HL_, WR=WR, WH=WH, WL=WL, SCB=SCB, JUNK=JUNK, NAR=NAR, AR=AR, MOD=MOD,
             ADAB=ADAB, NG=NG, IDN=IDN, ONE=ONE, EPSC=EPSC, SML=SML, R=R, NP=NP, psum=psum, XD=XD,
             sem=sem, sems=sems, esem=esem)
    plan, _ = _queues(T, I, out, phases, debug, None)
    _, (PE, SP, SA, DV, PO) = _queues(T, I, out, phases, debug, plan)
    block = stack.enter_context(nc.Block())
    block.tensor(lambda e: PE.emit(e))
    block.scalar(lambda e: SA.emit(e))
    block.vector(lambda e: DV.emit(e))
    block.gpsimd(lambda e: PO.emit(e))
    block.sync(lambda e: SP.emit(e))


def _queues(T, I, out, phases, debug, plan):
    YT, HH_, HL_, WR, WH, WL, SCB, JUNK = (T[n] for n in ("YT", "HH_", "HL_", "WR", "WH", "WL", "SCB", "JUNK"))
    NAR, AR, MOD, ADAB, NG, IDN, ONE = (T[n] for n in ("NAR", "AR", "MOD", "ADAB", "NG", "IDN", "ONE"))
    EPSC, SML, R, NP, psum, XD = (T[n] for n in ("EPSC", "SML", "R", "NP", "psum", "XD"))
    sem, sems, esem = T["sem"], T["sems"], T["esem"]
    lanes = [0]

    def lane():
        n = lanes[0]
        lanes[0] += 1
        if n == len(sems):
            sems.append(sem(f"lane{n}"))
        return [sems[n], 0]

    PE, SP = Queue(esem[0]), Queue(esem[1])
    SA, DV, PO = (Queue(n, serial=True) for n in esem[2:5])
    acc = Ring([Slot(p) for p in psum[0:4]])
    wrk = Ring([Slot(p) for p in psum[4:8]])
    wring = Ring([Slot(WR[:, i, :], lane()) for i in range(R)])

    def act(o, i, fn, *w, bias=None, scale=1.0, accum=None, chain=True):
        kw = {}
        if bias is not None:
            kw["bias"] = bias
        if accum is not None:
            kw["accum_out"] = accum
        return SA.op(lambda e: e.activation(o, i, fn, scale=scale, **kw), *w, chain=chain)

    def tt(o, a, b, op, *w, q=None, chain=True):
        return (q or DV).op(lambda e: e.tensor_tensor(o, a, b, op), *w, chain=chain)

    def ts(o, a, s1, s2, op0, op1, *w, q=None):
        if s2 is None:
            return (q or DV).op(lambda e: e.tensor_scalar(o, a, s1, None, op0), *w)
        return (q or DV).op(lambda e: e.tensor_scalar(o, a, s1, s2, op0, op1), *w)

    def stt(o, a, s, b, op0, op1, *w, chain=True):
        return DV.op(lambda e: e.scalar_tensor_tensor(out=o, in0=a, scalar=s, in1=b, op0=op0, op1=op1), *w,
                     chain=chain)

    def copy(o, a, *w, q=None):
        return (q or DV).op(lambda e: e.tensor_copy(o, a), *w)

    def recip(o, a, *w):
        return DV.op(lambda e: e.reciprocal(o, a), *w)

    def rmax(o, a, *w):
        return DV.op(lambda e: e.reduce_max(o, a, AX), *w)

    def rsum(o, a, *w):
        return DV.op(lambda e: e.reduce_sum(o, a, AX), *w)

    def mm(o, l, r, start, stop, *w, inc=False):
        return PE.op(lambda e: e.matmul(o, l, r, start=start, stop=stop), *w, inc=inc)

    def tr(o, i, *w, inc=False):
        k = i.shape[0]
        return PE.op(lambda e: e.transpose(o, i, IDN[0:k, 0:k]), *w, inc=inc)

    def load(pairs, *w):
        ln = lane()
        for o, name in pairs:
            t = PO.dma(o, I[name], ln, *w)
        return t

    mem = {"bar": []}

    def phase_begin(end=NAR - 1536):
        mem["at"], mem["end"] = 0, end
        mem["bar"] = [q.last() for q in (PE, SA, DV, PO)]

    def carve(size, shape=None, **kw):
        at = mem["at"]
        mem["at"] += size
        assert mem["at"] <= mem["end"], mem
        ap = AR[:, at:at + size]
        return ap.rearrange(shape, **kw) if shape else ap

    def slot(size, shape=None, **kw):
        s = Slot(carve(size, shape, **kw))
        s.free = list(mem["bar"])
        return s

    SQR = Ring([Slot(AR[:, NAR - 512 * (i + 1):NAR - 512 * i]) for i in range(2)])
    MOR = Ring([Slot(AR[:, NAR - 1024 + 256 * i:NAR - 768 + 256 * i]) for i in range(4)])
    RS = Slot(AR[:, NAR - 1536:NAR - 1024])
    RA = Slot(RS.ap[:, 256:512])

    tc0 = PO.op(lambda e: e.memset(ONE[:], 1.0))
    tc1 = PO.op(lambda e: e.memset(EPSC[:], EPS))
    t_c = load(((IDN[:], "ident"), (ADAB[:], "ada_b"), (NG[:], "norm_g")))
    xlane = lane()
    c2 = SML[:, 0:32]
    t_c2 = SP.dma(c2, I["c2"], lane())
    t_sc = SP.dma(SCB[:], I["cc"], lane())
    for n in range(NB):
        t_x = SA.dma(YT[:, n, :], I["xt"][n], xlane)
    for q in (PE, SA, DV):
        q.wait(tc0, tc1, t_c)

    t = act(SML[:, 32:64], c2, ACT.Tanh, t_c2, scale=0.5)
    t = stt(SML[:, 32:64], SML[:, 32:64], 1.0, c2, ALU.add, ALU.mult, t, t_c2)
    t_s2 = ts(c2, SML[:, 32:64], 0.5, None, ALU.mult, None, t)
    Uf = AR[:, 0:4096]
    Sf = SCB[:].rearrange("p a b -> p (a b)")
    t = act(Uf, Sf, ACT.Tanh, t_sc, scale=0.5)
    t_scb = stt(Sf, Uf, 1.0, Sf, ALU.add, ALU.mult, t, t_sc)

    xtok = [t_x] * NB
    htok = {}
    ytok = [None] * NB
    hfree = []
    xsrc = [I["xt"], None]
    stlane = lane()
    modtok = {}

    def ada_block(l, b):
        t = None
        for half in range(2):
            k = slice(1024 * half, 1024 * half + 1024)
            s, tl = tile(I["ada_w"][l, b, :, k])
            x = s.ap
            vs = (0, 1) if l != 3 else (0,)
            for v in vs:
                o = JUNK[:].bitcast(BF16)[:, 0:1024] if v != vs[-1] else x
                m = MOD[:, l, b, v:v + 1]
                t = DV.op(lambda e, v=v, o=o, m=m, x=x, k=k, half=half: e.tensor_tensor_reduce(
                    out=o, in0=x, in1=SCB[:, v, k], scale=0.5, scalar=m if half else 0.0,
                    op0=ALU.mult, op1=ALU.add, accum_out=m), tl, t_scb)
            give(s, t)
        return t

    def ada_finish(l, part, t):
        p = slice(16 * part, 16 * part + 16)
        for v in (0, 1) if l != 3 else (0,):
            t = tt(MOD[:, l, p, v], MOD[:, l, p, v], ADAB[:, l, p], ALU.add, t)
            if part == 1:
                t = stt(MOD[:, l, p, v], MOD[:, l, p, v], 1.0, NG[:, l, :], ALU.add, ALU.mult, t)
        modtok[l, part] = t

    def ada_start():
        ring = Ring([Slot(AR[:, 4096 + 1024 * i:5120 + 1024 * i], lane()) for i in range(5)])
        S2 = c2.rearrange("p (k v) -> p k v", v=2)
        bank = wrk.next()
        bw = bank.take()

        def pe_block(i):
            for half in range(2):
                s = ring.next()
                tl = SA.dma(s.ap, I["ada_p"][i, :, 1024 * half:1024 * half + 1024], s.lane, *s.take())
                w = s.ap.rearrange("p (k n) -> p k n", k=8)
                for k in range(8):
                    t = mm(bank.ap[:, 2 * i:2 * i + 2], w[:, k, :], S2[:, 8 * half + k, :],
                           half == 0 and k == 0, half == 1 and k == 7, tl, t_s2, *bw, inc=k == 7)
                    bw.clear()
                s.free = [t]
            return t

        rest = [16 + b for b in range(16)] + list(range(NPE, 16))
        x = list(range(NB))
        for i in range(NPE):
            tp = pe_block(i)
            for b in rest[2 * i:2 * i + 2]:
                tv = ada_block(0, b)
            for j in x[2 * i - 4:2 * i - 2] if i > 1 else ():
                square_sum(j, ALL, *square(j, ALL, xtok[j]))
        for b in rest[2 * NPE:]:
            tv = ada_block(0, b)
        tv = copy(MOD[:, 0, 0:NPE, :], bank.ap[:, 0:2 * NPE].rearrange("p (b v) -> p b v", v=2), tp)
        bank.free = [tv]
        ada_finish(0, 1, tv)
        ada_finish(0, 0, tv)

    def ada_thunks(l, parts=(0, 1, 2)):
        for part in parts:
            for b in range(16):
                def f(part=part, b=b):
                    t = ada_block(l, 16 * part + b)
                    if b == 15:
                        ada_finish(l, part, t)
                yield f

    background = []

    def bg(n=1):
        for _ in range(n):
            if background:
                background.pop(0)()

    used = []
    tiles = []
    pieces = {}
    pring = Ring([Slot((WH[:, i, :], WL[:, i, :])) for i in range(NP)])
    order = plan or []
    state = {"wide": True, "at": 0, "cut": 0, "split": 0, "cuts": 0}

    def fetch():
        while len(tiles) < len(order):
            ready = [s for s in wring.slots if s.free is not None]
            if not ready:
                return
            s = min(ready, key=lambda x: x.turn)
            wring.i += 1
            s.turn = wring.i
            tokens, s.free = s.free, None
            tiles.append((s, SP.dma(s.ap, order[len(tiles)][0], s.lane, *tokens)))

    def more_tiles(at, n, tokens):
        more = [Slot(AR[:, at + 1024 * i:at + 1024 * i + 1024], lane()) for i in range(n)]
        for s in more:
            s.free = list(tokens)
        wring.slots += more
        if plan is not None:
            fetch()
        return more

    def give(s, t):
        s.free = [t]
        if plan is not None:
            fetch()

    def cut(n):
        fetch()
        while state["cuts"] < n and state["cut"] < len(tiles):
            i = state["cut"]
            state["cut"] += 1
            if not order[i][1]:
                continue
            s, tw = tiles[i]
            p = pring.next()
            hi, lo = p.ap
            a = act(hi, s.ap, ACT.Copy, tw, *p.take())
            q = PO if state["wide"] or state["cuts"] % 2 else DV
            state["cuts"] += 1
            b = tt(lo, s.ap, hi.bitcast(F32), ALU.subtract, a, tw, q=q)
            pieces[i] = (p, b)
            give(s, b)

    def split_piece(src):
        used.append((src, True))
        if plan is None:
            return pring.slots[0], None
        i = state["at"]
        state["at"] += 1
        state["split"] += 1
        cut(state["split"] + NP - 1)
        return pieces[i]

    def split_tile(src):
        return [src[:, 0:1024], src[:, 1024:2048]]

    def tile(src):
        used.append((src, False))
        if plan is None:
            return wring.slots[0], None
        i = state["at"]
        state["at"] += 1
        fetch()
        state["cut"] = max(state["cut"], i + 1)
        return tiles[i]

    def triple(o, w, x, first, last, *tokens, inc):
        mm(o, w[0], x[0], first, False, *tokens)
        mm(o, w[0], x[1], False, False)
        return mm(o, w[1], x[0], False, last, inc=inc)

    def listed(t):
        return t if isinstance(t, list) else [t]

    def proj(src, rhs, rtok, cols, K=16):
        bank = acc.next()
        bw = bank.take()
        n = cols[1] - cols[0]
        for h in range(0, K, 16):
            js = split_tile(src[:, 128 * h:128 * h + 2048] if K > 16 else src)
            for half in range(2):
                p, tw = split_piece(js[half])
                w = [x.rearrange("p (k n) -> p k n", k=8) for x in p.ap]
                for k in range(8):
                    c = h + 8 * half + k
                    t = triple(bank.ap[:, 0:n], [x[:, k, :] for x in w], rhs(c), c == 0,
                               c == K - 1, tw, *listed(rtok[c]), *bw, inc=k == 7)
                    bw = []
                p.free = [t]
        return bank, t

    def hproj(src, cols=ALL):
        return proj(src, lambda k: (HH_[:, k, cols[0]:cols[1]], HL_[:, k, cols[0]:cols[1]]), htok,
                    cols)

    def tproj(src, cols):
        tbs = list(range(cols[0] // 128, cols[1] // 128))
        banks = [acc.next() for _ in tbs]
        bws = [b.take() for b in banks]
        for i in range(4):
            js = split_tile(src[i])
            for half in range(2):
                p, tw = split_piece(js[half])
                w = [x.rearrange("p (k n) -> p k n", n=512) for x in p.ap]
                for bi, tb in enumerate(tbs):
                    for k in range(2):
                        c = i * 4 + 2 * half + k
                        h = [x[:, c, 128 * tb:128 * tb + 128] for x in (HH_, HL_)]
                        ww = [x[:, k, :] for x in w]
                        t = triple(banks[bi].ap[:], h, ww, c == 0, c == 15, tw, *htok[c], *bws[bi],
                                   inc=k == 1)
                        bws[bi] = []
                p.free = [t]
        return banks, t

    stat = {}

    def square(j, cols, tok):
        a, b = cols
        s = SQR.next()
        return s, act(s.ap[:, 0:b - a], YT[:, j, a:b], ACT.Square, tok, *s.take())

    def square_sum(j, cols, s, tok):
        n = cols[1] - cols[0]
        r = RS if n == 512 else RA
        if j == 0:
            t = copy(r.ap[:, 0:n], s.ap[:, 0:n], tok, *r.take(), q=PO)
        else:
            t = tt(r.ap[:, 0:n], r.ap[:, 0:n], s.ap[:, 0:n], ALU.add, tok, q=PO)
        s.free = [t]
        if j == 15:
            bank = stat["bank"] = wrk.next()
            t = mm(bank.ap[:, 0:n], ONE[:], r.ap[:, 0:n], True, True, t, *bank.take(), inc=True)
            r.free = [t]
            stat["t"] = t

    def squares(cols):
        for j in range(NB):
            s, t = square(j, cols, xtok[j])
            square_sum(j, cols, s, t)

    def rstd(cols):
        n = cols[1] - cols[0]
        t = act(RS.ap[:, 0:n], stat["bank"].ap[:, 0:n], ACT.Sqrt, stat["t"], *RS.take(),
                bias=EPSC[:], scale=1.0 / 2048)
        stat["bank"].free = [t]
        return recip(RS.ap[:, 0:n], RS.ap[:, 0:n], t)

    def modnorm(l, cols):
        t_r = rstd(cols)
        cut(state["split"] + NP)
        a0 = cols[0]
        segs = [(c, v) for c, v in ((CTX, 1), (LAT, 0)) if a0 <= c[0]]
        w = list(hfree)
        late = []
        htok.clear()
        v_pool = lambda a: a == LAT[0] and len(segs) == 2

        def low(j, a, b, mo, sh, m, t2):
            if v_pool(a):
                t = tt(HL_[:, j, a:b], mo, HH_[:, j, a:b].bitcast(F32), ALU.subtract, t2, *w, q=PO,
                       chain=False)
            else:
                t = stt(HL_[:, j, a:b], mo, sh, HH_[:, j, a:b].bitcast(F32), ALU.add, ALU.subtract,
                        t2, *w, chain=False)
            htok.setdefault(j, []).append(t)
            m.free = [t]

        for j in range(NB):
            for (a, b), v in segs:
                m = MOR.next()
                mo = m.ap[:, 0:b - a]
                sh = MOD[:, l, j, v:v + 1]
                t = stt(mo, YT[:, j, a:b], MOD[:, l, 16 + j, v:v + 1],
                        RS.ap[:, a - a0:b - a0], ALU.mult, ALU.mult,
                        t_r, xtok[j], modtok[l, 1], *m.take(), chain=False)
                t2 = act(HH_[:, j, a:b], mo, ACT.Identity, t, modtok[l, 0], *w, bias=sh, chain=False)
                if v_pool(a):
                    t2 = act(mo, mo, ACT.Identity, bias=sh)
                late.append((j, a, b, mo, sh, m, t2))
                if len(late) > 2:
                    low(*late.pop(0))
        while late:
            low(*late.pop(0))
        RS.free = [t]
        yfree[:] = [DV.last(), xsrc[1]]
        return t

    def split_act(n, dst, src, *tokens, q=None):
        a = act(dst[0], src, ACT.Copy, *tokens)
        return tt(dst[1], src, dst[0].bitcast(F32), ALU.subtract, a, q=q or (PO if n % 3 == 2 else DV))

    ysplit = set()

    def split_y(ns, cols):
        a0, b0 = cols
        for n in ns:
            ytok[n] = split_act(n, (HH_[:, n, a0:b0], HL_[:, n, a0:b0]), YT[:, n, a0:b0], ytok[n],
                                *hfree)
            ysplit.add(n)

    def outproj(src, l, cols, half=False, sq=None):
        a0, b0 = cols
        sq = sq or cols
        for s in SQR.slots + [RS, RA]:
            s.free += [q.last() for q in (PE, SA, DV, PO)]
        more = more_tiles(0, 4, [q.last() for q in (PE, SA, DV, PO)])
        xlane_ = [lane() for _ in range(4)]
        xl = []
        hy = lambda k: (HH_[:, k, a0:b0], HL_[:, k, a0:b0])
        split_y([n for n in range(NB) if n not in ysplit], cols)
        ysplit.clear()
        hfree[:] = []
        late = []
        for n in range(NB):
            tx = SP.dma(YT[:, n, a0:b0], xsrc[0][n, :, a0:b0], xlane_[n % 4], ytok[n], xsrc[1],
                        *(xl[n - 4:n - 3] if n >= 4 else []))
            bank, t = proj(src[n], hy, ytok, cols)
            for (a, b), v in ((CTX, 1), (LAT, 0)):
                if a < a0:
                    continue
                if half:
                    td = stt(YT[:, n, a:b], bank.ap[:, a - a0:b - a0], 0.5, YT[:, n, a:b],
                             ALU.mult, ALU.add, t, tx)
                else:
                    td = stt(YT[:, n, a:b], bank.ap[:, a - a0:b - a0], MOD[:, l, 32 + n, v:v + 1],
                             YT[:, n, a:b], ALU.mult, ALU.add, t, modtok[l, 2], tx)
            bank.free = [td]
            xl.append(td)
            xtok[n] = td
            late.append((n, *square(n, sq, td)))
            if len(late) > 1:
                j, s, tq = late.pop(0)
                square_sum(j, sq, s, tq)
            bg(int(l == 0 and n % 4 == 0))
            if n == (11 if l == 0 else 8):
                del wring.slots[R:]
            if n >= 1:
                ts_ = SP.dma(XD[n - 1, :, a0:b0], YT[:, n - 1, a0:b0], stlane, xtok[n - 1])
            bg(1)
        ts_ = SP.dma(XD[NB - 1, :, a0:b0], YT[:, NB - 1, a0:b0], stlane, xtok[NB - 1])
        for j, s, tq in late:
            square_sum(j, sq, s, tq)
        assert all(s.free for s in more)
        hfree[:] = [PE.last()]
        xsrc[0], xsrc[1] = XD, ts_


    def gate_silu(bank, t, dst, cols, tmp, extra=()):
        n = cols[1] - cols[0]
        ta = act(tmp.ap[:, 0:n], bank.ap[:, 0:n], ACT.Tanh, t, *tmp.take(), scale=0.5)
        td = stt(dst, tmp.ap[:, 0:n], 1.0, bank.ap[:, 0:n], ALU.add, ALU.mult, ta, *extra)
        tmp.free = [td]
        bank.free = [td]
        return td

    def fnet(l, jj, cols):
        CT = carve(1536, "p (s c n) -> p s c n", s=3, c=2)
        tk = load(((CT, "dft_t"),), *mem["bar"])
        more_tiles(7008, 3, mem["bar"])
        ab = Ring([slot(4 * 514, "p (t s n) -> p t s n", t=4, s=2) for _ in range(2)])
        tmp = Ring([slot(512) for _ in range(2)])
        a0, b0 = cols
        tbs = list(range(a0 // 128, b0 // 128))
        zt = {}
        for i, s in enumerate(ab.slots):
            z1 = DV.op(lambda e, s=s: e.memset(s.ap[:, :, 1, 0:1], 0.0), *mem["bar"])
            z2 = DV.op(lambda e, s=s: e.memset(s.ap[:, :, 1, 256:257], 0.0))
            zt[id(s)] = z2
        for g in range(4):
            A = ab.next()
            aw = A.take()
            ev = []
            js = split_tile(I["dft_d"])
            banks = [wrk.next() for _ in tbs]
            bws = [b.take() for b in banks]
            for half in range(2):
                p, tw = split_piece(js[half])
                w = [x.rearrange("p (k n) -> p k n", n=512) for x in p.ap]
                for bi, tb in enumerate(tbs):
                    for k in range(2):
                        c = 4 * g + 2 * half + k
                        hs = [x[:, c, 128 * tb:128 * tb + 128] for x in (HH_, HL_)]
                        t = triple(banks[bi].ap[:], hs, [x[:, k, :] for x in w], c % 4 == 0,
                                   c % 4 == 3, tw, *htok[c], *bws[bi], inc=k == 1)
                        bws[bi] = []
                p.free = [t]
            for tb, bank in zip(tbs, banks):
                t1 = act(A.ap[:, tb, 0, :], bank.ap[:, 0:257], ACT.Copy, t, *aw)
                t2 = act(A.ap[:, tb, 1, 1:256], bank.ap[:, 257:512], ACT.Copy)
                bank.free = [t2]
                ev.append(t2)
            for b in range(4):
                n = 4 * g + b
                bank, t = hproj(I["f_gate"][jj, n], cols)
                ytok[n] = gate_silu(bank, t, YT[:, n, a0:b0], cols, tmp.next(), yfree)
                bg(1)
            if g == 3:
                hfree[:] = [PE.last()]
                split_y(range(12), cols)
            for b in range(4):
                n = 4 * g + b
                off = 128 * b if b < 2 else 1 + 128 * (b - 2)
                sg = 1 if b < 2 else 2
                bank = wrk.next()
                bw = bank.take()
                for si in range(len(tbs) // 2):
                    m = 0
                    for tc in range(2):
                        tb = tbs[2 * si + tc]
                        for s_, mat in ((0, 0), (1, sg)):
                            t = mm(bank.ap[:, 256 * si:256 * si + 256], A.ap[:, tb, s_, off:off + 128],
                                   CT[:, mat, tc, :], m == 0, m == 3, *ev, zt[id(A)], tk, *bw,
                                   inc=m == 3)
                            bw = []
                            m += 1
                td = tt(YT[:, n, a0:b0], bank.ap[:, 0:b0 - a0], YT[:, n, a0:b0], ALU.mult, t, ytok[n])
                bank.free = [td]
                ytok[n] = td
                if g < 3:
                    bg(1)
            A.free = [t]
        outproj(I["f_out"][jj], l, cols)

    yfree = []

    def mlstm(l):
        bar = list(mem["bar"])
        QK = Ring([slot(1024, "p (a n) -> p a n", a=2) for _ in range(2)])
        V = Ring([slot(4 * 257, "p (t n) -> p t n", t=4)])
        O = Ring([slot(1024, "p (t n) -> p t n", t=4)])
        C = carve(512)
        HH = slot(1024, "p (t n) -> p t n", t=4)
        pat = mem["at"]
        P = Ring([Slot(carve(1536)), Slot(carve(1536))])
        E2 = Ring([slot(512)])
        more_tiles(mem["at"], 1, bar)
        IG, LF, CU, MX = (AR[:, pat + 512 * i:pat + 512 * i + 512] for i in range(4))
        E1 = AR[:, pat + 2048:pat + 2560]
        ACOL = SML[:, 0:160].rearrange("p (t r) -> p t r", t=4)
        ECOL = SML[:, 160:320].rearrange("p (t r) -> p t r", t=4)
        GB = SML[:, 320:321]
        HN = SML[:, 321:337]
        ST = Ring([Slot(SML[:, 340 + 16 * i:356 + 16 * i]) for i in range(4)])
        t_g = load(((GB, "m_bg"), (HN, "m_hn")), *bar)
        t_hn = ts(HN, HN, 0.5, None, ALU.mult, None, t_g)
        for s in V.slots:
            t_one = DV.op(lambda e, s=s: e.memset(s.ap[:, :, 256:257], 1.0), *bar)
        bank, t = hproj(I["m_g"])
        r = slice(0, 40)
        a = act(IG[r], bank.ap[0:40, :], ACT.Identity, t, t_g, *bar, bias=GB[0:40])
        f = act(LF[r], bank.ap[64:104, :], ACT.Identity, bias=GB[64:104])
        bank.free = [f]
        e = act(E1[r], LF[r], ACT.Abs, f)
        e = act(E1[r], E1[r], ACT.Exp, e, scale=-1.0)
        e = act(E1[r], E1[r], ACT.Ln, e, bias=ONE[r, 0:1])
        t = ts(LF[r], LF[r], 0.0, None, ALU.min, None, e)
        t = tt(LF[r], LF[r], E1[r], ALU.subtract, t, e)
        z = DV.op(lambda e_: e_.memset(E1[r], 0.0), t)

        def scan(o, d1, op1, *w):
            t1 = DV.op(lambda e_: e_.tensor_tensor_scan(o[0:8], LF[0:8], d1[0:8], 0.0, ALU.add, op1), *w)
            t2 = DV.op(lambda e_: e_.tensor_tensor_scan(
                o[32:40, 0:256][:, ::-1], LF[32:40, 0:256][:, ::-1], d1[32:40, 0:256][:, ::-1],
                0.0, ALU.add, op1), *w)
            return DV.op(lambda e_: e_.tensor_tensor_scan(
                o[32:40, 256:512][:, ::-1], LF[32:40, 256:512][:, ::-1], d1[32:40, 256:512][:, ::-1],
                o[32:40, 0:1], ALU.add, op1), t2, t1)

        zc = DV.op(lambda e_: e_.memset(CU[r], 0.0), *bar)
        zm = DV.op(lambda e_: e_.memset(MX[r], 0.0), *bar)
        t_cu = scan(CU, E1, ALU.add, z, t, zc)
        t_mx = scan(MX, IG, ALU.max, t, a, zm)
        t_c = tt(C[r], CU[r], MX[r], ALU.subtract, t_cu, t_mx)
        t_a = tt(IG[r], IG[r], CU[r], ALU.subtract, t_cu, t_mx)
        t_e = act(MX[r], MX[r], ACT.Exp, t_c, scale=-1.0)
        bank = wrk.next()
        bw = bank.take()
        for tb in range(4):
            t = tr(bank.ap[:, 40 * tb:40 * tb + 40], IG[r, 128 * tb:128 * tb + 128], t_a, *bw)
            bw = []
        for tb in range(4):
            t = tr(bank.ap[:, 160 + 40 * tb:200 + 40 * tb], MX[r, 128 * tb:128 * tb + 128], t_e,
                   inc=tb == 3)
        t1 = copy(SML[:, 0:320], bank.ap[:, 0:320], t)
        bank.free = [t1]
        t_col = t1
        for s in P.slots:
            s.free = [t_a, t_e, t, t_c]

        heads = {}

        def project(h):
            qk, v, o = QK.next(), V.next(), O.next()
            qw = qk.take()
            st = heads[h] = dict(qk=qk, v=v, o=o)

            def q_():
                bank, t = hproj(I["m_q"][h])
                st["tq"] = act(qk.ap[:, 0, :], bank.ap[:], ACT.Copy, t, *qw, scale=float(128 ** -0.5))
                bank.free = [st["tq"]]

            def k_():
                bank, t = hproj(I["m_k"][h])
                st["tk"] = act(qk.ap[:, 1, :], bank.ap[:], ACT.Copy, t, *qw)
                bank.free = [st["tk"]]

            def vo():
                banks, t = tproj(I["m_vo"][h], ALL)
                vw, ow = v.take(), o.take()
                for tb, b in enumerate(banks):
                    t1 = act(o.ap[:, tb, :], b.ap[:, 256:512], ACT.Tanh, t, *ow, scale=0.5)
                    t2 = copy(v.ap[:, tb, 0:256], b.ap[:, 0:256], t, t1, t_one, *vw)
                    b.free = [t1, t2]
                st["tv"] = t2
                st["to"] = ts(o.ap[:], o.ap[:], 0.5, 0.5, ALU.mult, ALU.add, t1, q=PO)

            def z_(b):
                n = 2 * h + b
                bank, t = hproj(I["m_z"][n])
                ytok[n] = gate_silu(bank, t, YT[:, n, :], ALL, E2.next(), yfree)
            return [q_, k_, vo], [lambda: z_(0), lambda: z_(1)]

        fill = []

        def go(n=1):
            for _ in range(n):
                if fill:
                    fill.pop(0)()
                    bg(1)

        span = {(0, 0): (0, 512), (1, 0): (128, 512), (2, 0): (256, 512), (3, 0): (384, 512),
                (0, 1): None, (1, 1): (0, 512), (2, 1): (256, 384), (3, 1): (256, 512)}

        def attend(h):
            st = heads[h]
            qk, v, o = st["qk"], st["v"], st["o"]
            tcb = []
            cbs = []
            for d in range(2):
                bank = wrk.next()
                row = 32 * d + h
                t = mm(bank.ap[:], IDN[0:40, row:row + 1].to_broadcast([40, 128]), C[0:40, :],
                       True, True, t_c, *bank.take(), inc=True)
                bank.held = True
                cbs.append(bank)
                tcb.append(t)
            pcol = [0, 512, 1024, 1280]
            ptok = {}
            Ps = [P.next(), P.next()]
            Pw = [p.take() for p in Ps]
            for sbk in range(4):
                c0, c1 = (0, 512) if sbk < 2 else (256, 512)
                bank = wrk.next()
                t = mm(bank.ap[:, 0:c1 - c0], qk.ap[:, 1, 128 * sbk:128 * sbk + 128],
                       qk.ap[:, 0, c0:c1], True, True, st["tq"], st["tk"], *bank.take(), inc=True)
                if h < 7 or sbk in (0, 3):
                    go(1)
                fr = []
                for d in range(2):
                    p = Ps[d].ap[:, pcol[sbk]:pcol[sbk] + c1 - c0]
                    ta = ts(p, cbs[d].ap[:, c0:c1], ACOL[:, sbk, 32 * d + h:32 * d + h + 1], 0.0,
                            ALU.add, ALU.min, tcb[d], t_col, *Pw[d])
                    if sbk == 3:
                        cbs[d].free = [ta]
                        cbs[d].held = False
                    ta = act(p, p, ACT.Exp, ta)
                    g0 = 128 * sbk - c0
                    pd = p[:, g0:g0 + 128]
                    tm = PO.op(lambda e, pd=pd, sg=1 if d == 0 else -1: e.affine_select(
                        out=pd, in_=pd, compare_op=ALU.is_ge, fill=0.0, base=0,
                        pattern=[[sg, 128]], channel_multiplier=-sg), ta)
                    tm = tt(p, p, bank.ap[:, 0:c1 - c0], ALU.mult, tm, t)
                    ptok[sbk, d] = tm
                    fr.append(tm)
                bank.free = fr
            hw = HH.take()
            use = {0: ([0], [0, 1]), 1: ([0, 1], [1]), 2: ([0, 1, 2], [0, 1, 2, 3]),
                   3: ([0, 1, 2, 3], [0, 1, 3])}
            for tb in range(4):
                for d in range(2):
                    bank = wrk.next()
                    bw = bank.take()
                    ks = use[tb][d]
                    for i, s_ in enumerate(ks):
                        c = pcol[s_] + 128 * tb - (0 if s_ < 2 else 256)
                        t = mm(bank.ap[:, 0:257], Ps[d].ap[:, c:c + 128], v.ap[:, s_, :], i == 0,
                               i == len(ks) - 1, ptok[s_, d], st["tv"], *bw, inc=i == len(ks) - 1)
                        bw = []
                    Ps[d].free.append(t)
                    s = ST.next()
                    den = bank.ap[:, 256:257]
                    t1 = stt(s.ap[:, 0:1], den, -1.0, ECOL[:, tb, 32 * d + h:32 * d + h + 1],
                             ALU.mult, ALU.max, t, t_col, *s.take())
                    t1 = tt(s.ap[:, 0:1], den, s.ap[:, 0:1], ALU.max, t1)
                    t1 = recip(s.ap[:, 0:1], s.ap[:, 0:1], t1)
                    if d == 0:
                        t1 = ts(HH.ap[:, tb, :], bank.ap[:, 0:256], s.ap[:, 0:1], None, ALU.mult,
                                None, t1, *hw)
                    else:
                        t1 = stt(HH.ap[:, tb, :], bank.ap[:, 0:256], s.ap[:, 0:1], HH.ap[:, tb, :],
                                 ALU.mult, ALU.add, t1, th)
                    th = t1
                    s.free = [t1]
                    bank.free = [t1]
            v.free = [PE.last()]
            qk.free = [PE.last()]
            s = ST.next()
            ty = tt(HH.ap[:], HH.ap[:], o.ap[:], ALU.mult, th, st["to"])
            sq = E2.next()
            w = sq.take()
            for tb in range(4):
                t1 = act(sq.ap[:, 0:256], HH.ap[:, tb, :], ACT.Square, ty, *s.free, *w,
                         accum=s.ap[:, tb:tb + 1])
            sq.free = [t1]
            t1 = act(s.ap[:, 4:8], s.ap[:, 0:4], ACT.Sqrt, t1, bias=EPSC[:], scale=1.0 / 256)
            t1 = recip(s.ap[:, 4:8], s.ap[:, 4:8], t1)
            o.free = [ty]
            yn = []
            for tb in range(4):
                yn.append(ts(HH.ap[:, tb, :], HH.ap[:, tb, :], s.ap[:, 4 + tb:5 + tb], None,
                             ALU.mult, None, t1, sq.free[0]))
            s.free = [yn[-1]]
            go(1)
            for b in range(2):
                bank = wrk.next()
                bw = bank.take()
                for tb in range(4):
                    t = tr(bank.ap[:, 128 * tb:128 * tb + 128], HH.ap[:, tb, 128 * b:128 * b + 128],
                           yn[tb], *bw, inc=tb == 3)
                    bw = []
                n = 2 * h + b
                td = stt(YT[:, n, :], bank.ap[:], HN[:, n:n + 1], YT[:, n, :], ALU.mult, ALU.mult,
                         t, ytok[n], t_hn)
                bank.free = [td]
                ytok[n] = td
            HH.free = [t]

        first, z = project(0)
        fill += first
        go(9)
        for h in range(8):
            fill += z
            if h < 7:
                first, z = project(h + 1)
                fill += first
            attend(h)
            go(9)
        hfree[:] = [PE.last()]
        outproj(I["m_out"], l, ALL)

    def attn(l):
        bar = list(mem["bar"])
        VT = carve(2048, "p (t n) -> p t n", t=4)
        KT = carve(2048, "p (g n) -> p g n", g=4)
        QT = Ring([slot(512)])
        SQ, QG, RQ = slot(512), slot(512), slot(512)
        T1 = SQ
        PM = slot(1536)
        PT = slot(1536)
        TZ = slot(512)
        ROT = SML[:, 0:128]
        COS = carve(256)
        SIN = SML[:, 208:464]
        QN = SML[:, 128:130]
        ST = Ring([Slot(SML[:, 140 + 16 * i:156 + 16 * i]) for i in range(4)])
        tk = load(((ROT, "rot1"), (COS, "cos1"), (SIN, "sin1"), (QN, "qkn")), *bar)

        def rope_norm(bank, t, dst, gain, extra):
            t1 = act(SQ.ap, bank.ap[:], ACT.Square, t, *SQ.take())
            t2 = act(QG.ap, bank.ap[:], ACT.Copy, t, tk, *QG.take(), scale=gain)
            bank.free = [t2]
            b1, b2 = wrk.next(), wrk.next()
            t1 = mm(b1.ap[:], ONE[:], SQ.ap, True, True, t1, *b1.take(), inc=True)
            SQ.free = [t1]
            t3 = mm(b2.ap[:, 0:256], ROT, QG.ap[:, 256:512], True, True, t2, tk, *b2.take(), inc=True)
            t1 = act(RQ.ap, b1.ap[:], ACT.Sqrt, t1, *RQ.take(), bias=EPSC[:], scale=1.0 / 128)
            b1.free = [t1]
            t1 = recip(RQ.ap, RQ.ap, t1)
            t4 = tt(T1.ap[:, 0:256], b2.ap[:, 0:256], SIN, ALU.mult, t3, tk, *T1.take())
            b2.free = [t4]
            t5 = tt(QG.ap[:, 256:512], QG.ap[:, 256:512], COS, ALU.mult, t3)
            t5 = tt(QG.ap[:, 256:512], QG.ap[:, 256:512], T1.ap[:, 0:256], ALU.add, t4, t5)
            T1.free = [t5]
            t5 = tt(dst, QG.ap, RQ.ap, ALU.mult, t5, t1, *extra)
            QG.free = [t5]
            RQ.free = [t5]
            return t5

        banks, t = tproj(I["a_v"], ALL)
        for tb, b in enumerate(banks):
            tv = copy(VT[:, tb, :], b.ap[:], t, *bar)
            b.free = [tv]
        ktok = []
        for g in range(4):
            bank, t = hproj(I["a_k"][g])
            ktok.append(rope_norm(bank, t, KT[:, g, :], QN[:, 1:2], bar))
            bg(1)
        qs = {}
        fill = []

        def go(n=1):
            for _ in range(n):
                if fill:
                    fill.pop(0)()
                    bg(1)

        def project(h):
            def q_():
                bank, t = hproj(I["a_q"][h])
                q = QT.next()
                qs[h] = (q, rope_norm(bank, t, q.ap, QN[:, 0:1], q.take()))

            def z_():
                bank, t = hproj(I["a_z"][h])
                ytok[h] = gate_silu(bank, t, YT[:, h, :], ALL, TZ, yfree)
            return q_, z_

        sc = float(128 ** -0.5)
        where = {0: (0, 256), 1: (256, 256), 2: (512, 512), 3: (1024, 512)}

        def attend(h):
            g = h // 4
            q, tq = qs[h]
            pw = PM.take()
            b0 = wrk.next()
            bw = b0.take()
            for tb in range(2):
                t = mm(b0.ap[:, 256 * tb:256 * tb + 256], q.ap[:, 128 * tb:128 * tb + 128],
                       KT[:, g, 0:256], True, True, tq, ktok[g], *bw, inc=True)
                bw = []
            bs = [(b0, 0, t), (b0, 256, t)]
            for tb in (2, 3):
                b = wrk.next()
                t = mm(b.ap[:], q.ap[:, 128 * tb:128 * tb + 128], KT[:, g, :], True, True, *b.take(),
                       inc=True)
                bs.append((b, 0, t))
            q.free = [t]
            pt = []
            for tb in range(4):
                b, c0, t = bs[tb]
                at, n = where[tb]
                s = ST.next()
                sa = s.ap
                t1 = rmax(sa[:, 0:1], b.ap[:, c0:c0 + n], t, *s.take())
                t1 = ts(sa[:, 1:2], sa[:, 0:1], -sc, None, ALU.mult, None, t1)
                t1 = act(PM.ap[:, at:at + n], b.ap[:, c0:c0 + n], ACT.Exp, t1, *pw, bias=sa[:, 1:2],
                         scale=sc, accum=sa[:, 2:3])
                b.free = [t1]
                t2 = recip(sa[:, 3:4], sa[:, 2:3], t1)
                t2 = ts(PM.ap[:, at:at + n], PM.ap[:, at:at + n], sa[:, 3:4], None, ALU.mult, None, t2)
                s.free = [t2]
                pt.append(t2)
            go(1)
            pw = PT.take()
            te = []
            for i in range(3):
                b = wrk.next()
                bw = b.take()
                if i < 2:
                    jobs = [(tb, i) for tb in range(4)]
                else:
                    jobs = [(2, 2), (3, 2), (2, 3), (3, 3)]
                for m, (tb, s_) in enumerate(jobs):
                    at = where[tb][0] + 128 * s_
                    t = tr(b.ap[:, 128 * m:128 * m + 128], PM.ap[:, at:at + 128], pt[tb], *bw,
                           inc=m == 3)
                    bw = []
                if i % 2:
                    te.append(act(PT.ap[:, 512 * i:512 * i + 512], b.ap[:], ACT.Copy, t, *pw))
                else:
                    te.append(copy(PT.ap[:, 512 * i:512 * i + 512], b.ap[:], t, *pw))
                b.free = [te[-1]]
            PM.free = [t]
            go(1)
            b = wrk.next()
            bw = b.take()
            for s_ in range(4):
                vv = VT[:, s_, 128 * g:128 * g + 128]
                if s_ < 2:
                    o_, r_ = b.ap[:], PT.ap[:, 512 * s_:512 * s_ + 512]
                else:
                    o_, r_ = b.ap[:, 256:512], PT.ap[:, 512 + 256 * s_:768 + 256 * s_]
                t = mm(o_, vv, r_, s_ == 0, s_ == 3, *te, tv, *bw, inc=s_ == 3)
                bw = []
            PT.free = [t]
            td = stt(YT[:, h, :], b.ap[:], 0.5, YT[:, h, :], ALU.mult, ALU.mult, t, ytok[h])
            b.free = [td]
            ytok[h] = td

        q_, z_ = project(0)
        fill.append(q_)
        go(9)
        for h in range(16):
            if h < 15:
                nq, nz = project(h + 1)
                fill.append(nq)
            fill.append(z_)
            z_ = nz
            attend(h)
            go(9)
        hfree[:] = [PE.last()]
        outproj(I["a_out"], l, ALL, sq=LAT)

    def gainnorm(cols, gain, tg, dst):
        t_r = rstd(cols)
        cut(state["split"] + NP)
        a, b = cols
        toks = []
        w = list(hfree)
        late = []

        def low(j, hi, lo, mo, m, t2):
            toks[j] = tt(lo, mo, hi.bitcast(F32), ALU.subtract, t2, *w, q=PO if j % 2 else DV,
                         chain=False)
            m.free = [toks[j]]

        for j in range(NB):
            m = MOR.next() if dst else None
            mo = m.ap[:, 0:b - a] if dst else YT[:, j, a:b]
            t = stt(mo, YT[:, j, a:b], gain[:, j:j + 1], RS.ap[:, 0:b - a],
                    ALU.mult, ALU.mult, t_r, tg, xtok[j], *(m.take() if dst else [xsrc[1]]), chain=False)
            toks.append(t)
            if not dst:
                square_sum(j, cols, *square(j, cols, t))
            else:
                hi, lo = dst(j)
                late.append((j, hi, lo, mo, m, act(hi, mo, ACT.Copy, t, *w,
                                                        chain=False)))
                if len(late) > 2:
                    low(*late.pop(0))
        while late:
            low(*late.pop(0))
        RS.free = [t]
        if dst:
            yfree[:] = [DV.last(), xsrc[1]]
        return toks

    GN = SML[:, 592:640]

    def nsa():
        phase_begin(NAR)
        bar = list(mem["bar"])
        a0, b0 = LAT
        c = LAT
        QB = carve(2048, "p (n t) -> p n t", n=8)
        KD = [carve(1024, "p (g t) -> p g t", g=4) for _ in range(2)]
        T2K, T2V = KD
        VV = carve(1024, "p (t n) -> p t n", t=2)
        COS, SIN = carve(256), carve(256)
        SQ, QG, RQ = slot(256), slot(256), slot(256)
        T1 = SQ
        pmat = mem["at"]
        PM = slot(1024)
        CMP = carve(480, "p (t n) -> p t n", t=2)
        POOLW = Ring([slot(272) for _ in range(3)])
        OT = slot(256)
        WHO = carve(1024, "p (n e) -> p n e", n=8)
        PL = MC[:, 0:2048].rearrange("p (n t) -> p n t", n=8)
        PT = slot(1024, "p (a n) -> p a n", a=4)
        KR = Ring([Slot(PT.ap[:, 2 * i:2 * i + 2, :]) for i in range(2)])
        for s in KR.slots:
            s.free = list(bar)
        KC = SML[:, 0:60]
        VC = SML[:, 60:316].rearrange("p (g d) -> p g d", g=4)
        CST = carve(272)
        KN = SML[:, 316:320]
        PSC = SML[:, 320:336]
        GT = SML[:, 336:432].rearrange("p (t n) -> p t n", t=2)
        W2 = AR[:, pmat:pmat + 384]
        POS = AR[:, pmat + 384:pmat + 416].rearrange("p (a j) -> p a j", a=2)
        ST = Ring([Slot(SML[:, 432 + 16 * i:448 + 16 * i]) for i in range(8)])
        HID = [AR[:, pmat + 416 + 120 * i:pmat + 536 + 120 * i].rearrange("p (b n) -> p b n", b=2)
               for i in range(2)]
        B64, ROT = CST[:, 0:128], CST[:, 128:256]
        INV = CST[:, 256:257]
        tk = load(((CST[:, 0:257], "nsa_c"), (KN, "nsa_kn"), (PSC, "pool_s"), (WHO, "w_ho")), *bar)
        PI_ = PM.ap[:, 0:256].bitcast(I32)
        PF, KF, RR = PM.ap[:, 256:512], PM.ap[:, 512:768], PM.ap[:, 768:1024]
        t = load(((PI_, "positions"),), *bar)
        t = copy(PF, PI_, t)
        t = ts(PF, PF, INV, None, ALU.mult, None, t)
        t = ts(PI_, PF, float(1 / (2 * np.pi)), None, ALU.mult, None, t)
        t = copy(KF, PI_, t)
        t = stt(RR, KF, -TWO_PI_A, PF, ALU.mult, ALU.add, t)
        t = stt(RR, KF, -TWO_PI_B, RR, ALU.mult, ALU.add, t)
        t = stt(RR, KF, -TWO_PI_C, RR, ALU.mult, ALU.add, t)
        PIF = 3.1415925
        t = ts(RR, RR, PIF, -PIF, ALU.min, ALU.max, t)
        t_s = act(SIN, RR, ACT.Sin, t)
        t = act(KF, RR, ACT.Abs, t)
        t = ts(KF, KF, -1.0, float(np.pi / 2), ALU.mult, ALU.add, t)
        t_cs = act(COS, KF, ACT.Sin, t)
        t_w2 = load(((W2, "w2"), (POS, "pos")), t_cs)
        CC = [carve(60, "p (g n) -> p g n", g=4) for _ in range(2)]
        for g in range(4):
            tcc = copy(CC[0][:, g, :], COS[:, 31::16], t_cs, t_s, *bar)
            tcc = copy(CC[1][:, g, :], SIN[:, 31::16])

        def rope_norm(src, sfree, t, dst, gain, extra, n=256, cs=None):
            co, si = cs or (COS, SIN)
            t1 = act(SQ.ap[:, 0:n], src, ACT.Square, t, *SQ.take())
            t2 = act(QG.ap[:, 0:n], src, ACT.Copy, t, tk, *QG.take(), scale=gain)
            if sfree is not None:
                sfree.free = [t2]
            b1, b2 = wrk.next(), wrk.next()
            t1 = mm(b1.ap[:, 0:n], B64, SQ.ap[:, 0:n], True, True, t1, tk, *b1.take(), inc=True)
            SQ.free = [t1]
            t3 = mm(b2.ap[:, 0:n], ROT, QG.ap[:, 0:n], True, True, t2, tk, *b2.take(), inc=True)
            t1 = act(RQ.ap[:, 0:n], b1.ap[:, 0:n], ACT.Sqrt, t1, *RQ.take(), bias=EPSC[:],
                     scale=1.0 / 64)
            b1.free = [t1]
            t1 = recip(RQ.ap[:, 0:n], RQ.ap[:, 0:n], t1)
            t4 = tt(T1.ap[:, 0:n], b2.ap[:, 0:n], si, ALU.mult, t3, t_cs, t_s, tcc, *T1.take())
            b2.free = [t4]
            t5 = tt(QG.ap[:, 0:n], QG.ap[:, 0:n], co, ALU.mult, t3)
            t5 = tt(QG.ap[:, 0:n], QG.ap[:, 0:n], T1.ap[:, 0:n], ALU.add, t4, t5)
            T1.free = [t5]
            t5 = tt(dst, QG.ap[:, 0:n], RQ.ap[:, 0:n], ALU.mult, t5, t1, *extra)
            QG.free = [t5]
            RQ.free = [t5]
            return t5

        t2tok = []
        for i, (name, T2) in enumerate((("n_kc", T2K), ("n_vc", T2V))):
            dlane = lane()
            kr = KR.next()
            kw = kr.take()
            for b in range(2):
                bank, t = hproj(I[name][b], c)
                t1 = copy(kr.ap[:, b, :], bank.ap[:, 0:256], t, *kw)
                bank.free = [t1]
            for par in range(2):
                td = PO.dma(T2[0:64, par::2, :], kr.ap[64 * par:64 * par + 64, :, :], dlane, t1, *bar)
                td = PO.dma(T2[64:128, par::2, 0:255], kr.ap[64 * par:64 * par + 64, :, 1:256], dlane)
            kr.free = [td]
            t2tok.append(td)
        for n in range(4):
            bank, t = hproj(I["n_q"][n], c)
            tq = rope_norm(bank.ap[:, 0:256], bank, t, QB[:, n, :], KN[:, 0:1], bar)
        MV, t_mv = [], []
        for i, T2 in enumerate((T2K, T2V)):
            m = YT[:, 8 + 2 * i:10 + 2 * i, :].rearrange("p a b -> p (a b)")[:, 0:976]
            m = m.rearrange("p (j n) -> p j n", j=16)
            for u in range(2):
                for g in range(4):
                    src = T2[:, g, :].rearrange("p (m r) -> p m r", r=16)[:, u:u + 15, 0:16:2]
                    dst = m[:, 8 * u:8 * u + 8, 15 * g:15 * g + 15].rearrange("p r n -> p n r")
                    t = copy(dst, src, t2tok[i], *yfree)
            t = copy(m[:, :, 60:61], POS[:, i, :].rearrange("p (j a) -> p j a", a=1), t_w2)
            MV.append(m)
            t_mv.append(t)
        for n in range(4, 8):
            bank, t = hproj(I["n_q"][n], c)
            tq = rope_norm(bank.ap[:, 0:256], bank, t, QB[:, n, :], KN[:, 0:1], bar)
        banks, t = tproj(I["n_v"], c)
        for tb, b in enumerate(banks):
            tv = copy(VV[:, tb, :], b.ap[:], t, *bar)
            b.free = [tv]
        bank, t = hproj(I["n_g"], c)
        gtmp = POOLW.slots[1]
        t = act(gtmp.ap[0:48, 0:256], bank.ap[0:48, 0:256], ACT.Tanh, t, *gtmp.take(), scale=0.5)
        bank.free = [t]
        t = ts(gtmp.ap[0:48, 0:256], gtmp.ap[0:48, 0:256], 0.5, 0.5, ALU.mult, ALU.add, t)
        bank = wrk.next()
        bw = bank.take()
        for tb in range(2):
            t2 = tr(bank.ap[:, 48 * tb:48 * tb + 48], gtmp.ap[0:48, 128 * tb:128 * tb + 128], t, *bw,
                    inc=tb == 1)
            bw = []
        t_gt = copy(SML[:, 336:432], bank.ap[:, 0:96], t2, *bar)
        bank.free = [t_gt]
        gtmp.free = [t2]
        ktok = []
        for i, name in enumerate(("n_ks", "n_kw")):
            dlane = lane()
            kr = KR.next()
            kw = kr.take()
            for b in range(2):
                bank, t = hproj(I[name][b], c)
                t1 = rope_norm(bank.ap[:, 0:256], bank, t, kr.ap[:, b, :], KN[:, 2 + i:3 + i], kw)
            for par in range(2):
                for half in range(2):
                    td = PO.dma(KD[i][64 * half:64 * half + 64, par::2, :],
                                kr.ap[64 * par:64 * par + 64, :, :], dlane, t1, DV.last())
            kr.free = [td]
            ktok.append(td)
        PT.free = [s.free[0] for s in KR.slots]
        for i in range(2):
            for hb in range(2):
                bank = acc.next()
                bw = bank.take()
                for half in range(2):
                    s, tw = tile(split_tile(I["n_w1"][i, hb])[half])
                    w = s.ap.rearrange("p (k n) -> p k n", k=8)
                    for k in range(8):
                        j = 8 * half + k
                        tm_ = mm(bank.ap[:, 0:61], w[:, k, :], MV[i][:, j, :], j == 0, j == 15, t_mv[i], tw,
                                 *bw, inc=k == 7)
                        bw = []
                    give(s, tm_)
                st = ST.next()
                ta = act(st.ap[:, 0:1], bank.ap[:, 60:61], ACT.Copy, tm_, *st.take())
                hd = HID[i][:, hb, :]
                x1 = T1.ap[:, 0:60]
                tb_ = ts(x1, bank.ap[:, 0:60], st.ap[:, 0:1], None, ALU.add, None, ta, *T1.take())
                bank.free = [tb_]
                st.free = [tb_]
                ta = act(hd, x1, ACT.Tanh, tb_, t_cs, scale=0.5)
                ta = stt(hd, hd, 1.0, x1, ALU.add, ALU.mult, ta)
                T1.free = [ta]
            if i == 0:
                bank = acc.next()
                bw = bank.take()
                for hb in range(2):
                    t = mm(bank.ap[:, 0:60], W2[:, 128 * hb:128 * hb + 128], HID[0][:, hb, :], hb == 0,
                           hb == 1, ta, t_w2, *bw, inc=hb == 1)
                    bw = []
                x1 = POOLW.slots[0]
                t = act(x1.ap[:, 0:60], bank.ap[:, 0:60], ACT.Copy, t, *x1.take(), scale=0.5)
                bank.free = [t]
                fl = lambda z: z.rearrange("p g n -> p (g n)")
                t_kc = rope_norm(x1.ap[:, 0:60], x1, t, KC, KN[:, 1:2], bar, n=60,
                                 cs=(fl(CC[0]), fl(CC[1])))
            else:
                bank = acc.next()
                bw = bank.take()
                for g in range(4):
                    for hb in range(2):
                        t = mm(bank.ap[0:15, 64 * g:64 * g + 64], HID[1][:, hb, 15 * g:15 * g + 15],
                               W2[:, 256 + 64 * hb:320 + 64 * hb], hb == 0, hb == 1, ta, t_w2, *bw,
                               inc=hb == 1)
                        bw = []
                t_vc = act(SML[0:15, 60:316], bank.ap[0:15, 0:256], ACT.Copy, t, *bar, scale=0.5)
                bank.free = [t_vc]
        mvread = PE.last()
        PM.free = [mvread]
        t_q = tq

        fill = []

        def go(n=1):
            for _ in range(n):
                if fill:
                    fill.pop(0)()

        mtok = [[None] * NB, [None] * NB]
        pltok = [None] * 8

        def merge(n, w):
            def f():
                bank, t = hproj(I["n_m"][16 * w + n], c)
                o = YT[:, n, 256:512] if w == 0 else YT[:, n, 0:256]
                mtok[w][n] = act(o, bank.ap[:, 0:256], ACT.Tanh, t, mvread, *yfree, scale=0.5)
                bank.free = [mtok[w][n]]
            return f

        def pool(n):
            def f():
                bank, t = hproj(I["n_p"][n], c)
                steps = n // 2 + 1
                u, a, b = POOLW.slots
                w = u.take() + a.take() + b.take()
                t1 = PO.op(lambda e: e.memset(u.ap[:, 0:16], 0.0), *w)
                t2 = PO.op(lambda e: e.memset(a.ap[:, 0:16], 0.0))
                t3 = PO.op(lambda e: e.memset(b.ap[:, 0:16], 0.0))
                t = copy(u.ap[:, 16:272], bank.ap[:, 0:256], t, *w)
                bank.free = [t]
                cur, k = u, 1
                for i in range(steps):
                    nxt = a if i % 2 == 0 else b
                    t = tt(nxt.ap[:, 16:272], cur.ap[:, 16:272], cur.ap[:, 16 - k:272 - k], ALU.add,
                           t, t1, t2, t3, q=PO)
                    cur, k = nxt, 2 * k
                t = tt(cur.ap[:, 16:272], cur.ap[:, 16:272], CNT(n // 2), ALU.mult, t, t_cm[0], q=PO)
                t = tt(PL[:, n, :], cur.ap[:, 16:272], u.ap[:, 16:272], ALU.subtract, t, *bar, q=PO)
                for s in POOLW.slots:
                    s.free = [t]
                pltok[n] = t
            return f

        def poolout(n):
            def f():
                g = n // 4
                s, tw = None, None
                if n % 4 == 0:
                    pw["s"], pw["t"] = tile(split_tile(I["w_pool"][n // 8])[n // 4 % 2])
                s, tw = pw["s"], pw["t"]
                w = s.ap.rearrange("p (n k e) -> p n k e", n=4, k=2)
                bank = acc.next()
                bw = bank.take()
                for k in range(2):
                    t = mm(bank.ap[:, 0:256], w[:, n % 4, k, :], PL[:, 2 * g + k, :], k == 0, k == 1,
                           pltok[2 * g + k], tw, *bw, inc=k == 1)
                    bw = []
                if n % 4 == 3:
                    give(s, t)
                x = QG
                t = act(x.ap, bank.ap[:, 0:256], ACT.Copy, t, tk, *x.take(), scale=PSC[:, n:n + 1])
                bank.free = [t]
                t = stt(YT[:, n, 0:256], YT[:, n, 0:256], 1.0, x.ap, ALU.add, ALU.mult, t, mtok[1][n])
                x.free = [t]
                mtok[1][n] = t
            return f

        pw = {}
        for n in range(8):
            fill.append(merge(2 * n, 0))
            fill.append(merge(2 * n + 1, 0))
            fill.append(pool(n))
        for n in range(16):
            fill += [merge(n, 1), poolout(n)]
        ow = {}

        isc = 0.125
        M3 = lambda ap: ap.rearrange("p (h n) -> p h n", h=16)
        for tb in range(2):
            banks = [wrk.next(), wrk.next()]
            pc = CMP[:, tb, :]
            for par in range(2):
                bw = banks[par].take()
                b = 64 * par
                for i in range(8):
                    g = i // 2
                    t = mm(banks[par].ap[:, 15 * i:15 * i + 15],
                           QB[b:b + 64, i, 128 * tb:128 * tb + 128],
                           KC[b:b + 64, 15 * g:15 * g + 15], True, True, t_q, t_kc, *bw, inc=i == 7)
                    bw = []
                t = tt(CMP[:, tb, 120 * par:120 * par + 120], banks[par].ap[:, 0:120],
                       CMADD(tb)[:, 0:120], ALU.add, t, t_cm[0])
                banks[par].free = [t]
            go(2)
            s = T1.ap[:, 0:16]
            t = rmax(s, M3(pc), t, *T1.take())
            t = tt(M3(pc), M3(pc), s.rearrange("p (h a) -> p h a", a=1).to_broadcast([128, 16, 15]),
                   ALU.subtract, t)
            t = act(pc, pc, ACT.Exp, t, scale=isc)
            t = rsum(s, M3(pc), t)
            t = recip(s, s, t)
            for par in range(2):
                t = tt(s[:, 8 * par:8 * par + 8], s[:, 8 * par:8 * par + 8], GT[:, tb, 3 * par:48:6],
                       ALU.mult, t, t_gt)
            t = tt(M3(pc), M3(pc), s.rearrange("p (h a) -> p h a", a=1).to_broadcast([128, 16, 15]),
                   ALU.mult, t)
            t = tt(pc, pc, CMMUL(tb), ALU.mult, t)
            T1.free = [t]
            t_cmp = t

        def attend(h):
            g, b, blk = h // 4, 64 * (h % 2), h // 2
            ch = 8 * (h % 2) + h // 2
            P = PM.ap.rearrange("p (t x) -> p t x", t=2)
            pw_ = PM.take()
            toks = []
            sbank = []
            for tb in range(2):
                n = 128 * (tb + 1)
                bank = wrk.next()
                bw = bank.take()
                for br in range(2):
                    t = mm(bank.ap[:, n * br:n * br + n], QB[b:b + 64, blk, 128 * tb:128 * tb + 128],
                           KD[br][b:b + 64, g, 0:n], True, True, t_q, ktok[br], *bw, inc=br == 1)
                    bw = []
                sbank.append((bank, t))
            exps = []
            for tb in range(2):
                n = 128 * (tb + 1)
                bank, t = sbank[tb]
                pp = P[:, tb, 0:2 * n]
                t = tt(pp, bank.ap[:, 0:2 * n], MASK(tb), ALU.add, t, t_cm[0], *pw_)
                bank.free = [t]
                s = ST.next()
                sa = s.ap
                t = rmax(sa[:, 0:2], pp.rearrange("p (r n) -> p r n", r=2), t, *s.take())
                t = ts(sa[:, 2:4], sa[:, 0:2], -isc, None, ALU.mult, None, t)
                for br in range(2):
                    t1 = act(P[:, tb, n * br:n * br + n], P[:, tb, n * br:n * br + n], ACT.Exp, t,
                             bias=sa[:, 2 + br:3 + br], scale=isc, accum=sa[:, 4 + br:5 + br])
                exps.append((tb, n, s, sa, t1))
            for tb, n, s, sa, t1 in exps:
                t = recip(sa[:, 6:8], sa[:, 4:6], t1)
                t = tt(sa[:, 6:8], sa[:, 6:8], GT[:, tb, 3 * h + 1:3 * h + 3], ALU.mult, t, t_gt)
                for br in range(2):
                    t1 = ts(P[:, tb, n * br:n * br + n], P[:, tb, n * br:n * br + n],
                            sa[:, 6 + br:7 + br], None, ALU.mult, None, t)
                s.free = [t1]
                toks.append(t1)
            go(2)
            A, B = wrk.next(), wrk.next()
            aw, bw = A.take(), B.take()
            for br in range(2):
                tr(A.ap[:, 256 * br:256 * br + 128], P[:, 0, 128 * br:128 * br + 128], toks[0], *aw)
                aw = []
                t = tr(A.ap[:, 256 * br + 128:256 * br + 256], P[:, 1, 256 * br:256 * br + 128],
                       toks[1], inc=br == 1)
            ta_ = t
            for br in range(2):
                t = tr(B.ap[:, 128 * br:128 * br + 128], P[:, 1, 256 * br + 128:256 * br + 256], *bw)
                bw = []
            for tb in range(2):
                t = tr(B.ap[0:15, 256 + 128 * tb:384 + 128 * tb], CMP[:, tb, 15 * ch:15 * ch + 15],
                       t_cmp, inc=tb == 1)
            PM.free = [t]
            X = PT.ap
            xw = PT.take()
            t1 = act(X[:, 0:2, :], A.ap.rearrange("p (a b) -> p a b", a=2), ACT.Copy, ta_, *xw)
            t2 = copy(X[:, 2, :], B.ap[:, 0:256], t, *xw)
            t3 = copy(X[0:15, 3, :], B.ap[0:15, 256:512])
            A.free, B.free = [t1], [t3]
            go(1)
            if h % 2 == 0:
                ow["bank"] = acc.next()
                bw = ow["bank"].take()
                ow["bank"].held = True
            else:
                bw = []
            ob = ow["bank"].ap
            for br in range(2):
                mm(ob[b:b + 64, 0:256], VV[:, 0, 256 * br + 64 * g:256 * br + 64 * g + 64],
                   X[:, br, :], br == 0, False, t1, t3, tv, *bw)
                bw = []
                mm(ob[b:b + 64, 128:256], VV[:, 1, 256 * br + 64 * g:256 * br + 64 * g + 64],
                   X[:, 2, 128 * br:128 * br + 128], False, False)
            t = mm(ob[b:b + 64, 0:256], VC[0:15, g, :], X[0:15, 3, :], False, True, t_vc, inc=True)
            PT.free = [t]
            if h % 2:
                t = copy(OT.ap, ob[:, 0:256], t, *OT.take())
                ow["bank"].free = [t]
                ow["bank"].held = False
                for i in range(2):
                    hh = h - 1 + i
                    bank = wrk.next()
                    tm_ = mm(bank.ap[:, 0:256], WHO[64 * i:64 * i + 64, blk, :],
                             OT.ap[64 * i:64 * i + 64, :], True, True, t, tk, *bank.take(), inc=True)
                    OT.free = [tm_]
                    td = stt(YT[:, hh, 256:512], YT[:, hh, 256:512], 1.0, bank.ap[:, 0:256],
                             ALU.add, ALU.mult, tm_, mtok[0][hh])
                    bank.free = [td]
                    mtok[0][hh] = td
            if h % 4 == 0:
                go(1)

        for h in range(16):
            attend(h)
        go(99)
        hfree[:] = [PE.last()]
        for n in range(16):
            ytok[n] = tt(YT[:, n, 256:512], YT[:, n, 256:512], YT[:, n, 0:256], ALU.add, mtok[0][n],
                         mtok[1][n])
            split_y([n], LAT)
        outproj(I["n_out"], None, LAT, half=True)

    t_cm = [None]
    MC = SCB[:].rearrange("p a b -> p (a b)")
    MK = JUNK[:]

    def CMADD(tb):
        return MC[:, 3072 + 240 * tb:3312 + 240 * tb]

    def CMMUL(tb):
        return MC[:, 3552 + 240 * tb:3792 + 240 * tb]

    def CNT(i):
        return MC[:, 2048 + 256 * i:2304 + 256 * i]

    def MASK(tb):
        return MK[:, 0:512] if tb else MK[:, 512:768]

    def load_masks():
        w = [q.last() for q in (PE, SA, DV, PO)]
        t_cm[0] = load(((MC[:, 3072:3552], "cm_add"), (MC[:, 3552:4032], "cm_mul"),
                        (MC[:, 2048:3072], "cnt"), (MK[:, 0:768], "masks")), *w)

    def moe():
        phase_begin()
        bar = list(mem["bar"])
        c = LAT
        FH, FL = (x[:].rearrange("p a (b n) -> p (a b) n", n=256) for x in (HH_, HL_))
        pair = lambda k: (FH[:, k, :], FL[:, k, :])
        mproj = lambda src: proj(src, pair, htok, c)
        LG = carve(256)
        RB = SML[:, 0:1]
        CMB = carve(32, "p (t e) -> p t e", t=2)
        CR = carve(256)
        CBC = Ring([slot(256), slot(256)])
        TG = Ring([slot(256), slot(256)])
        UU = Ring([slot(256), slot(256)])
        IDX = SML[:, 4:8]
        S = SML[:, 16:96]
        t_b = load(((RB, "r_b"), (IDX, "idx4")), *bar)
        bank, t = mproj(I["r_w"])
        t = act(LG[0:20], bank.ap[0:20, 0:256], ACT.Identity, t, t_b, *bar, bias=RB[0:20])
        bank.free = [t]
        bank = wrk.next()
        bw = bank.take()
        for tb in range(2):
            t2 = tr(bank.ap[:, 20 * tb:20 * tb + 20], LG[0:20, 128 * tb:128 * tb + 128], t, *bw,
                    inc=tb == 1)
            bw = []
        LT = carve(40, "p (t n) -> p t n", t=2)
        t = copy(AR[:, mem["at"] - 40:mem["at"]], bank.ap[:, 0:40], t2)
        bank.free = [t]

        def products(n):
            return *mproj(I["e_g"][n // 2, n % 2]), *mproj(I["e_u"][n // 2, n % 2])

        early = [products(n) for n in range(2)]

        def first_max(oh, x, m, tmp, mt, t):
            t = yield ts(oh, x, m, None, ALU.is_equal, None, t)
            t = yield tt(tmp, oh, IDX, ALU.mult, t)
            t = yield rmax(mt, tmp, t)
            t = yield ts(oh, tmp, mt, None, ALU.is_equal, None, t)
            return t

        def choose(tb, t):
            G = LT[:, tb, 0:4]
            v = lambda a, n: S[:, 40 * tb + a:40 * tb + a + n]
            t = yield rmax(v(0, 1), G, t)
            t = yield ts(v(1, 1), v(0, 1), -1.0, None, ALU.mult, None, t)
            t = yield act(v(4, 4), G, ACT.Exp, t, bias=v(1, 1), accum=v(2, 1))
            t = yield recip(v(3, 1), v(2, 1), t)
            t = yield rmax(v(0, 1), v(4, 4), t)
            t = yield from first_max(v(8, 4), v(4, 4), v(0, 1), v(12, 4), v(1, 1), t)
            t = yield ts(v(16, 4), LT[:, tb, 4:8], v(8, 1), None, ALU.mult, None, t)
            for g in range(1, 4):
                t = yield stt(v(16, 4), LT[:, tb, 4 + 4 * g:8 + 4 * g], v(8 + g, 1), v(16, 4), ALU.mult,
                        ALU.add, t)
            t = yield rmax(v(0, 1), v(16, 4), t)
            t = yield from first_max(v(20, 4), v(16, 4), v(0, 1), v(12, 4), v(1, 1), t)
            t = yield stt(v(24, 4), v(20, 4), -1e30, v(16, 4), ALU.mult, ALU.add, t)
            t = yield rmax(v(28, 1), v(24, 4), t)
            t = yield from first_max(v(32, 4), v(24, 4), v(28, 1), v(12, 4), v(1, 1), t)
            t = yield tt(v(29, 1), v(28, 1), v(0, 1), ALU.subtract, t)
            t = yield act(v(29, 1), v(29, 1), ACT.Exp, t)
            t = yield ts(v(30, 1), v(29, 1), 1.0, None, ALU.add, None, t)
            t = yield recip(v(30, 1), v(30, 1), t)
            t = yield tt(v(30, 1), v(30, 1), v(3, 1), ALU.mult, t)
            t = yield tt(v(31, 1), v(30, 1), v(29, 1), ALU.mult, t)
            t = yield ts(v(36, 4), v(20, 4), v(30, 1), None, ALU.mult, None, t)
            t = yield stt(v(36, 4), v(32, 4), v(31, 1), v(36, 4), ALU.mult, ALU.add, t)
            for g in range(4):
                t = yield ts(CMB[:, tb, 4 * g:4 * g + 4], v(36, 4), v(8 + g, 1), None, ALU.mult, None, t)
            return t

        DV.serial = SA.serial = False
        chains = [(tb, choose(tb, t)) for tb in range(2)]
        t_ch = [next(g) for _, g in chains]
        while chains:
            for tb, g in list(chains):
                try:
                    t_ch[tb] = g.send(t_ch[tb])
                except StopIteration:
                    chains.remove((tb, g))
        DV.serial = SA.serial = True
        bank = wrk.next()
        bw = bank.take()
        for tb in range(2):
            t2 = tr(bank.ap[0:16, 128 * tb:128 * tb + 128], CMB[:, tb, :], *t_ch, *bw, inc=tb == 1)
            bw = []
        t_cr = copy(CR[0:16], bank.ap[0:16, 0:256], t2)
        bank.free = [t_cr]
        order_ = {"e": {}}
        hw = list(hfree)

        def spread(e):
            b = wrk.next()
            t = mm(b.ap[:, 0:256], IDN[0:16, e:e + 1].to_broadcast([16, 128]), CR[0:16, :], True,
                   True, t_cr, *b.take(), inc=True)
            s = CBC.next()
            t = act(s.ap, b.ap[:, 0:256], ACT.Copy, t, *s.take())
            b.free = [t]
            order_["e"][e] = (s, t)

        def expert(n, gb, tg, ub, tu):
            e, f = n // 2, n % 2
            if f == 0:
                spread(e)
            s, tc = order_["e"][e]
            g, u = TG.next(), UU.next()
            ta = act(g.ap, gb.ap[:, 0:256], ACT.Tanh, tg, *g.take(), scale=0.5)
            t1 = stt(g.ap, g.ap, 1.0, gb.ap[:, 0:256], ALU.add, ALU.mult, ta)
            gb.free = [t1]
            t2 = tt(u.ap, ub.ap[:, 0:256], s.ap, ALU.mult, tu, tc, *u.take())
            ub.free = [t2]
            if n < 16:
                t3 = tt(g.ap, g.ap, u.ap, ALU.mult, t1, t2)
                ytok2[n] = split_act(n, pair(16 + n), g.ap, t3, *hw, q=DV)
                u.free = [t3]
                g.free = [ytok2[n]]
            else:
                t3 = tt(YT[:, n - 16, 0:256], g.ap, u.ap, ALU.mult, t1, t2, *yfree)
                g.free, u.free = [t3], [t3]
                ytok2[n] = t3
            if f == 1:
                s.free = [t2]

        for n in range(32):
            expert(n, *(early[n] if n < 2 else products(n)))
        t = PE.last()
        for n in range(16, 32):
            ytok2[n] = split_act(n, pair(n - 16), YT[:, n - 16, 0:256], ytok2[n], t)
        down = lambda k: pair(16 + k) if k < 16 else pair(k - 16)
        xl_ = [lane() for _ in range(4)]
        tds = []
        for n in range(NB):
            tx = SP.dma(YT[:, n, 256:512], xsrc[0][n, :, 256:512], xl_[n % 4], xsrc[1], *yfree,
                        *(tds[n - 4:n - 3] if n >= 4 else []))
            bank, t = proj(I["e_d"][n], down, ytok2, c, K=32)
            td = stt(YT[:, n, 256:512], bank.ap[:, 0:256], 0.5, YT[:, n, 256:512], ALU.mult, ALU.add,
                     t, tx)
            bank.free = [td]
            tds.append(td)
            outs.append(SA.dma(out[n], YT[:, n, 256:512], olane, td))

    ytok2 = [None] * 32
    olane = lane()
    outs = []

    def settle(l):
        while background and (l, 1) not in modtok:
            bg(1)

    if "ada0" in phases:
        ada_start()
        background.extend(ada_thunks(0, (2,)))
        for l in (1, 2, 3):
            background.extend(ada_thunks(l))
    elif debug:
        for l in [l for l, p in enumerate(("fnet0", "mlstm", "attn", "fnet3")) if p in phases]:
            for f in ada_thunks(l):
                f()
    first = phases[0] if phases[0] != "ada0" else phases[1]
    if "ada0" not in phases:
        squares(ALL if first in ("fnet0", "mlstm", "attn") else LAT)
    if "fnet0" in phases:
        phase_begin()
        modnorm(0, ALL)
        fnet(0, 0, ALL)
    if "mlstm" in phases:
        settle(1)
        phase_begin()
        modnorm(1, ALL)
        mlstm(1)
    if "attn" in phases:
        settle(2)
        phase_begin()
        modnorm(2, ALL)
        attn(2)
    state["wide"] = False
    if "fnet3" in phases:
        settle(3)
        phase_begin()
        modnorm(3, LAT)
        fnet(3, 1, LAT)
    lat = lambda j: (HH_[:, j, 256:512], HL_[:, j, 256:512])
    if "nsa" in phases:
        load_masks()
        tg = load(((GN, "gains"),), *[q.last() for q in (PE, SA, DV, PO)])
        if "final" in phases:
            xtok[:] = gainnorm(LAT, GN[:, 0:16], tg, None)
            for n in range(NB):
                ts_ = SP.dma(XD[n, :, 256:512], YT[:, n, 256:512], stlane, xtok[n])
            xsrc[0], xsrc[1] = XD, ts_
        for j, t in enumerate(gainnorm(LAT, GN[:, 16:32], tg, lat)):
            htok[j] = [t]
        nsa()
    if "moe" in phases:
        tg = load(((GN, "gains"),), *[q.last() for q in (PE, SA, DV, PO)])
        FH, FL = (x[:].rearrange("p a (b n) -> p (a b) n", n=256) for x in (HH_, HL_))
        for j, t in enumerate(gainnorm(LAT, GN[:, 32:48], tg, lambda j: (FH[:, j, :], FL[:, j, :]))):
            htok[j] = [t]
        moe()
    elif debug:
        for n in range(NB):
            outs.append(SA.dma(out[n], YT[:, n, 256:512], olane, xtok[n]))
    if debug == "ctx":
        for n in range(NB):
            outs.append(SA.dma(I["dbg"][n], YT[:, n, 0:256], olane, xtok[n]))
    SP.wait(xsrc[1])
    SA.wait(outs[-1])

    return used, (PE, SP, SA, DV, PO)


def _blocks(w, n=128):
    k, m = w.shape
    return np.ascontiguousarray(w.reshape(k // 128, 128, m // n, n).transpose(2, 1, 0, 3)).reshape(
        m // n, 128, k // 128 * n)


def _wide(w):
    return _blocks(np.concatenate([w, np.zeros((w.shape[0], 128 - w.shape[1]), w.dtype)], 1))[0]


def _rows(w, kk=4):
    k, m = w.shape
    return np.ascontiguousarray(w.reshape(k // 128 // kk, kk, 128, m).transpose(0, 2, 1, 3)).reshape(
        k // 128 // kk, 128, kk * m)


def _col(v):
    v = v.reshape(v.shape[:-1] + (v.shape[-1] // 128, 128))
    return np.ascontiguousarray(np.moveaxis(v, -1, 0))


def _fourier_order():
    one = np.concatenate([np.arange(256), 511 - np.arange(256)])
    return np.concatenate([512 * g + one for g in range(4)])


def _constants():
    C = {}
    f = np.float32
    C["ident"] = np.eye(128, dtype=f)
    d = np.arange(512)[:, None]
    cosd = np.cos(2 * np.pi * ((d * np.arange(257)) % 512) / 512) / np.sqrt(512)
    sind = np.sin(2 * np.pi * ((d * np.arange(1, 256)) % 512) / 512) / np.sqrt(512)
    cd = np.concatenate([cosd, sind], 1).reshape(4, 128, 512).transpose(1, 0, 2).reshape(128, 2048)
    C["dft_d"] = np.ascontiguousarray(cd).astype(f)
    t = np.arange(256)
    ph = 2 * np.pi * (np.outer(t, t) % 256) / 256
    ct, st = np.cos(ph) / 32, np.sin(ph) / 32
    m = np.stack([ct, -st, st]).reshape(3, 2, 128, 256).transpose(2, 0, 1, 3)
    C["dft_t"] = np.ascontiguousarray(m).astype(f)
    r = np.zeros((128, 128), f)
    for i in range(64):
        r[2 * i + 1, 2 * i] = -1
        r[2 * i, 2 * i + 1] = 1
    C["rot1"] = r
    freqs = f(10000.0) ** (-np.arange(0, 64, 2, dtype=f) / f(64))
    rr = np.repeat(np.arange(4), 64).astype(f)
    cc = np.tile(np.arange(64), 4).astype(f)
    ang = np.concatenate([rr[:, None] * freqs, cc[:, None] * freqs], -1)
    C["cos1"] = np.ascontiguousarray(np.repeat(np.cos(ang), 2, axis=1).T).astype(f)
    C["sin1"] = np.ascontiguousarray(np.repeat(np.sin(ang), 2, axis=1).T).astype(f)
    nc_ = np.zeros((128, 257), f)
    nc_[0:64, 0:64] = 1
    nc_[64:128, 64:128] = 1
    for b in (0, 64):
        for i in range(8):
            nc_[b + 8 + i, 128 + b + i] = -1
            nc_[b + i, 128 + b + 8 + i] = 1
    inv = f(500000.0) ** (-np.arange(0, 16, 2, dtype=f) / f(16))
    for b in (0, 64):
        nc_[b:b + 8, 256] = inv
        nc_[b + 8:b + 16, 256] = inv
    C["nsa_c"] = nc_
    tt_ = np.arange(256).reshape(2, 128).T
    ok = (np.arange(15) * 16 + 31)[None, None, :] <= tt_[:, :, None]
    C["cm_add"] = np.tile(np.where(ok, 0.0, -1e30), (1, 1, 16)).astype(f)
    C["cm_mul"] = np.tile(ok, (1, 1, 16)).astype(f)
    C["cnt"] = np.broadcast_to(np.stack([1.0 / np.minimum(t + 1, w) for w in (2, 4, 8, 16)]),
                               (128, 4, 256)).astype(f)
    p = np.arange(128)[:, None]
    low = np.where(np.arange(128)[None] <= p, 0.0, -1e30)
    full = np.zeros((128, 128))
    C["masks"] = np.concatenate([full, low, full, low, low, low], 1).astype(f)
    C["idx4"] = np.broadcast_to(np.array([4.0, 3.0, 2.0, 1.0], f), (128, 4)).copy()
    return {k: np.ascontiguousarray(v) for k, v in C.items()}


def layout(x, c, ctx, c_ctx, ada_w, ada_b, norm_g, fnet_w_gate, fnet_w_out, mlstm_w_in,
           mlstm_b_gate, mlstm_hn, mlstm_w_out, attn_w_in, attn_qn, attn_kn, attn_w_out, final_g,
           positions_2, attn_norm_g_2, w_in_2, q_norm_g_2, k_norm_cmp_g_2, k_norm_slc_g_2,
           k_norm_swa_g_2, cmp_pos_emb_k_2, cmp_w1_k_2, cmp_w2_k_2, cmp_pos_emb_v_2, cmp_w1_v_2,
           cmp_w2_v_2, w_head_out_2, w_pool_2, pool_scale_2, w_out_2, ffn_norm_g_2,
           w_router_group_2, b_router_group_2, w_router_expert_2, b_router_expert_2,
           w_expert_gate_2, w_expert_up_2, w_expert_down_2):
    A = _constants()
    con = np.ascontiguousarray
    xt = np.concatenate([ctx[0], x[0]], 0)
    A["xt"] = con(xt.T.reshape(16, 128, 512))
    A["cc"] = con(np.broadcast_to(np.stack([c[0], c_ctx]), (128, 2, 2048)))
    A["ada_w"] = con(ada_w.transpose(0, 2, 1).reshape(4, 48, 128, 2048))
    A["ada_p"] = _blocks(ada_w[0][:, 0:128 * NPE])
    A["c2"] = con(np.stack([c[0], c_ctx]).reshape(2, 16, 128).transpose(2, 1, 0).reshape(128, 32))
    A["ada_b"] = _col(ada_b)
    A["norm_g"] = _col(norm_g)
    o = _fourier_order()
    A["f_gate"] = np.stack([_blocks(w[:, o]) for w in fnet_w_gate])
    A["f_out"] = np.stack([_blocks(w[o]) for w in fnet_w_out])
    w = mlstm_w_in[0]
    A["m_q"] = _blocks(w[:, 0:1024])
    A["m_k"] = _blocks(w[:, 1024:2048])
    v, og = w[:, 2048:4096], w[:, 4096:6144]
    A["m_vo"] = np.stack([_rows(np.concatenate([v[:, 256 * h:256 * h + 256],
                                                og[:, 256 * h:256 * h + 256]], 1)) for h in range(8)])
    g = w[:, 6144:6176]
    gp = np.zeros((2048, 128), w.dtype)
    bp = np.zeros((128, 1), mlstm_b_gate.dtype)
    for at, src in ((0, 0), (64, 8), (32, 16), (96, 24)):
        gp[:, at:at + 8] = g[:, src:src + 8]
        bp[at:at + 8, 0] = mlstm_b_gate[0, src:src + 8]
    A["m_g"] = _blocks(gp)[0]
    A["m_bg"] = bp
    A["m_z"] = _blocks(w[:, 6176:])
    A["m_hn"] = _col(mlstm_hn[0])
    A["m_out"] = _blocks(mlstm_w_out[0])
    w = attn_w_in[0]
    A["a_q"] = _blocks(w[:, 0:2048])
    A["a_k"] = _blocks(w[:, 2048:2560])
    A["a_v"] = _rows(w[:, 2560:3072])
    A["a_z"] = _blocks(w[:, 3072:])
    A["qkn"] = con(np.stack([attn_qn[0], attn_kn[0]], 1))
    A["a_out"] = _blocks(attn_w_out[0])
    A["gains"] = con(np.concatenate([_col(final_g), _col(attn_norm_g_2[0]), _col(ffn_norm_g_2[0])], 1))
    w = w_in_2[0]
    at = [0]

    def cut(n):
        at[0] += n
        return w[:, at[0] - n:at[0]]

    A["n_q"] = _blocks(cut(1024))
    A["n_kc"], A["n_vc"] = _blocks(cut(256)), _blocks(cut(256))
    ks, vs, kw, vw = cut(256), cut(256), cut(256), cut(256)
    A["n_ks"], A["n_kw"] = _blocks(ks), _blocks(kw)
    A["n_v"] = _rows(np.concatenate([vs, vw], 1))
    A["n_g"] = _wide(cut(48))
    A["n_p"] = _blocks(cut(1024))
    A["n_m"] = _blocks(cut(4096))
    two = lambda v_: np.concatenate([v_, v_])
    A["nsa_kn"] = con(np.stack([two(q_norm_g_2[0]), two(k_norm_cmp_g_2[0]), two(k_norm_slc_g_2[0]),
                                two(k_norm_swa_g_2[0])], 1))
    A["positions"] = con(np.broadcast_to(positions_2, (128, 256)))
    A["pos"] = con(np.stack([p_[0].reshape(16, 128).T for p_ in (cmp_pos_emb_k_2, cmp_pos_emb_v_2)], 1))
    A["n_w1"] = np.stack([_blocks(w_[0]) for w_ in (cmp_w1_k_2, cmp_w1_v_2)])
    k2 = cmp_w2_k_2[0].reshape(2, 128, 64)
    v2 = cmp_w2_v_2[0].reshape(2, 128, 64)
    A["w2"] = con(np.concatenate([k2[0], k2[0], k2[1], k2[1], v2[0], v2[1]], 1))
    A["w_ho"] = con(w_head_out_2[0].reshape(8, 128, 128).transpose(1, 0, 2))
    wp = w_pool_2[0].reshape(4, 2, 128, 4, 128)
    A["w_pool"] = con(wp.transpose(0, 3, 2, 1, 4).reshape(2, 8, 128, 2, 128).transpose(0, 2, 1, 3, 4)
                      .reshape(2, 128, 2048))
    A["pool_s"] = _col(pool_scale_2[0])
    A["n_out"] = _blocks(w_out_2[0])
    A["r_w"] = _wide(np.concatenate([w_router_group_2[0], w_router_expert_2[0]], 1))
    rb = np.zeros((128, 1), b_router_group_2.dtype)
    rb[0:4, 0] = b_router_group_2[0]
    rb[4:20, 0] = b_router_expert_2[0]
    A["r_b"] = rb
    A["e_g"] = np.stack([_blocks(w_) for w_ in w_expert_gate_2[0]])
    A["e_u"] = np.stack([_blocks(w_) for w_ in w_expert_up_2[0]])
    A["e_d"] = _blocks(w_expert_down_2[0].reshape(4096, 2048))
    return A


def kernel(**inputs):
    import concourse.bacc as _bacc
    from concourse.bass_utils import run_bass_kernel_spmd as _run

    arrays = layout(**{k: np.asarray(v) for k, v in inputs.items()})
    nc = _bacc.Bacc("TRN2", target_bir_lowering=False, num_devices=1)
    aps = {k: nc.dram_tensor(k, a.shape, mybir.dt.from_np(a.dtype), kind="ExternalInput").ap()
           for k, a in arrays.items()}
    out = nc.dram_tensor("out", (16, 128, 256), F32, kind="ExternalOutput").ap()
    program(nc, aps, out)
    r = _run(nc, [arrays], core_ids=[0])
    y = r.results[0]["out"]
    return np.ascontiguousarray(y.reshape(2048, 256).T)[None]
```
